# Optimizing a Trainium2 kernel written in Bass

```python
import jax, jax.numpy as jnp
from jax import lax
import numpy as np

D_MODEL = 1024
BATCH = 1
SEQ = 256
DEPTH = 1

GDN_HEADS = 4
GDN_DK = 128
GDN_DV = 128
ML_HEADS = 4
ML_DK = 128
ML_DV = 128
CONV_WIDTH = 4
CHUNK = 64
GATE_SOFTCAP = 15.0
N_EXPERTS = 32
TOP_K = 4
D_EXPERT = 1024
SWIGLU_LIMIT = 7.0
SWIGLU_ALPHA = 1.702
EXPERT_BLOCK = 256
NORM_EPS = 1e-6

GDN_QK = GDN_HEADS * GDN_DK
GDN_V = GDN_HEADS * GDN_DV
ML_QK = ML_HEADS * ML_DK
ML_V = ML_HEADS * ML_DV
IN_WIDTHS = (GDN_QK, GDN_QK, GDN_V, GDN_V, GDN_HEADS, GDN_HEADS,
             ML_QK, ML_QK, ML_V, ML_V, ML_HEADS, ML_HEADS,
             D_MODEL, D_MODEL)
D_IN = sum(IN_WIDTHS)
SPLIT_POINTS = [int(s) for s in np.cumsum(IN_WIDTHS)[:-1]]

kernel_name = "hybrid_gdn_mlstm_moe_block"

def rms_norm(x, g):
    xf = x.astype(jnp.float32)
    y = xf * lax.rsqrt(jnp.mean(xf * xf, axis=-1, keepdims=True) + NORM_EPS)
    return (y * g.astype(jnp.float32)).astype(x.dtype)

def head_rms_norm(x, g):
    return x * lax.rsqrt(jnp.mean(x * x, axis=-1, keepdims=True) + NORM_EPS) * g

def l2_normalize(x):
    return x * lax.rsqrt(jnp.sum(x * x, axis=-1, keepdims=True) + NORM_EPS)

def soft_cap(x):
    return GATE_SOFTCAP * jnp.tanh(x / GATE_SOFTCAP)

def causal_depthwise_conv(x, w):
    c = x.shape[-1]
    return lax.conv_general_dilated(
        x, w[:, None, :].astype(x.dtype), window_strides=(1,),
        padding=[(CONV_WIDTH - 1, 0)], dimension_numbers=("NWC", "WIO", "NWC"),
        feature_group_count=c)

def to_chunks(x, n_heads):
    b, s, hd = x.shape
    return x.reshape(b, s // CHUNK, CHUNK, n_heads, hd // n_heads).transpose(0, 3, 1, 2, 4)

def scalar_to_chunks(x):
    b, s, h = x.shape
    return x.reshape(b, s // CHUNK, CHUNK, h).transpose(0, 3, 1, 2)

def from_chunks(x):
    b, h, nc, c, d = x.shape
    return x.transpose(0, 2, 3, 1, 4).reshape(b, nc * c, h * d)

def causal_masks():
    idx = jnp.arange(CHUNK)
    return idx[:, None] > idx[None, :], idx[:, None] >= idx[None, :]

def gated_delta_rule(q, k, v, g, beta):
    strict, incl = causal_masks()
    gam = jnp.cumsum(g, axis=-1)
    decay = jnp.exp(jnp.where(incl, gam[..., :, None] - gam[..., None, :], -jnp.inf))
    kb = k * beta[..., None]
    lower = jnp.where(strict, jnp.einsum("bhnid,bhnjd->bhnij", kb, k) * decay, 0.0)
    eye = jnp.eye(CHUNK, dtype=q.dtype)
    dv = v.shape[-1]
    rhs = jnp.concatenate([v * beta[..., None], kb * jnp.exp(gam)[..., None]], axis=-1)
    sol = lax.linalg.triangular_solve(lower + eye, rhs, left_side=True, lower=True,
                                      unit_diagonal=True)
    u_local, w_state = sol[..., :dv], sol[..., dv:]
    attn = jnp.einsum("bhnid,bhnjd->bhnij", q, k) * decay
    q_dec = q * jnp.exp(gam)[..., None]
    gam_last = gam[..., -1]
    k_dec = k * jnp.exp(gam_last[..., None] - gam)[..., None]

    def step(state, inp):
        u0, w_c, qd, kd, a, gl = inp
        u = u0 - jnp.einsum("bhck,bhkv->bhcv", w_c, state)
        o = jnp.einsum("bhck,bhkv->bhcv", qd, state) + jnp.einsum("bhij,bhjv->bhiv", a, u)
        state = state * jnp.exp(gl)[..., None, None] + jnp.einsum("bhck,bhcv->bhkv", kd, u)
        return state, o

    b, h, _, _, dk = q.shape
    s0 = jnp.zeros((b, h, dk, dv), q.dtype)
    xs = tuple(jnp.moveaxis(t, 2, 0) for t in (u_local, w_state, q_dec, k_dec, attn, gam_last))
    _, o = lax.scan(step, s0, xs)
    return jnp.moveaxis(o, 0, 2)

def mlstm_chunkwise(q, k, v, i_pre, logf):
    _, incl = causal_masks()
    b_cum = jnp.cumsum(logf, axis=-1)
    d_log = jnp.where(incl, b_cum[..., :, None] - b_cum[..., None, :] + i_pre[..., None, :], -jnp.inf)
    m_loc = jnp.max(d_log, axis=-1)
    p = jnp.exp(d_log - m_loc[..., None]) * jnp.einsum("bhnid,bhnjd->bhnij", q, k)
    num_loc = jnp.einsum("bhnij,bhnjv->bhniv", p, v)
    den_loc = jnp.sum(p, axis=-1)
    b_last = b_cum[..., -1]
    a_log = b_last[..., None] - b_cum + i_pre
    m_chunk = jnp.max(a_log, axis=-1)
    wk = k * jnp.exp(a_log - m_chunk[..., None])[..., None]
    dc = jnp.einsum("bhnck,bhncv->bhnkv", wk, v)
    dn = jnp.sum(wk, axis=-2)

    def step(carry, inp):
        c_st, n_st, m_st = carry
        q_c, b_c, ml_c, num_c, den_c, dc_c, dn_c, bl_c, mc_c = inp
        m_inter = b_c + m_st[..., None]
        m_t = jnp.maximum(ml_c, m_inter)
        s_inter = jnp.exp(m_inter - m_t)
        s_loc = jnp.exp(ml_c - m_t)
        num = (s_inter[..., None] * jnp.einsum("bhck,bhkv->bhcv", q_c, c_st)
               + s_loc[..., None] * num_c)
        den = s_inter * jnp.einsum("bhck,bhk->bhc", q_c, n_st) + s_loc * den_c
        h = num / jnp.maximum(jnp.abs(den), jnp.exp(-m_t))[..., None]
        m_new = jnp.maximum(bl_c + m_st, mc_c)
        s_old = jnp.exp(bl_c + m_st - m_new)
        s_new = jnp.exp(mc_c - m_new)
        c_st = s_old[..., None, None] * c_st + s_new[..., None, None] * dc_c
        n_st = s_old[..., None] * n_st + s_new[..., None] * dn_c
        return (c_st, n_st, m_new), h

    b, h, _, _, dk = q.shape
    dv = v.shape[-1]
    carry0 = (jnp.zeros((b, h, dk, dv), q.dtype), jnp.zeros((b, h, dk), q.dtype),
              jnp.zeros((b, h), q.dtype))
    xs = tuple(jnp.moveaxis(t, 2, 0) for t in
               (q, b_cum, m_loc, num_loc, den_loc, dc, dn, b_last, m_chunk))
    _, hs = lax.scan(step, carry0, xs)
    return jnp.moveaxis(hs, 0, 2)

def token_mixer(h, w_in, gdn_conv, gdn_a_log, gdn_dt_bias, gdn_norm, ml_conv, ml_b_i, ml_b_f,
                ml_norm, w_up_gdn, w_up_ml, w_out):
    f32 = jnp.float32
    dt = h.dtype
    proj = (h @ w_in).astype(f32)
    (g_q, g_k, g_v, g_z, g_a, g_b, m_q, m_k, m_v, m_o, m_i, m_f,
     gate_gdn, gate_ml) = jnp.split(proj, SPLIT_POINTS, axis=-1)

    qkv = jax.nn.silu(causal_depthwise_conv(jnp.concatenate([g_q, g_k, g_v], axis=-1),
                                            gdn_conv.astype(f32)))
    a_q, a_k, a_v = jnp.split(qkv, [GDN_QK, 2 * GDN_QK], axis=-1)
    a_q = l2_normalize(to_chunks(a_q, GDN_HEADS)) * GDN_DK ** -0.5
    a_k = l2_normalize(to_chunks(a_k, GDN_HEADS))
    a_v = to_chunks(a_v, GDN_HEADS)
    log_decay = (-jnp.exp(gdn_a_log.astype(f32))[:, None, None]
                 * jax.nn.softplus(scalar_to_chunks(g_a) + gdn_dt_bias.astype(f32)[:, None, None]))
    beta = jax.nn.sigmoid(scalar_to_chunks(g_b))
    o_a = gated_delta_rule(a_q, a_k, a_v, log_decay, beta)
    o_a = from_chunks(head_rms_norm(o_a, gdn_norm.astype(f32))) * jax.nn.silu(g_z)

    qk = jax.nn.silu(causal_depthwise_conv(jnp.concatenate([m_q, m_k], axis=-1),
                                           ml_conv.astype(f32)))
    b_q, b_k = jnp.split(qk, [ML_QK], axis=-1)
    b_q = to_chunks(b_q, ML_HEADS)
    b_k = to_chunks(b_k, ML_HEADS) * ML_DK ** -0.5
    b_v = to_chunks(m_v, ML_HEADS)
    i_pre = soft_cap(scalar_to_chunks(m_i) + ml_b_i.astype(f32)[:, None, None])
    f_pre = soft_cap(scalar_to_chunks(m_f) + ml_b_f.astype(f32)[:, None, None])
    o_b = mlstm_chunkwise(b_q, b_k, b_v, i_pre, jax.nn.log_sigmoid(f_pre))
    o_b = from_chunks(head_rms_norm(o_b, ml_norm.astype(f32).reshape(ML_HEADS, 1, 1, ML_DV)))
    o_b = o_b * jax.nn.sigmoid(m_o)

    y_a = (o_a.astype(dt) @ w_up_gdn).astype(f32)
    y_b = (o_b.astype(dt) @ w_up_ml).astype(f32)
    y = jax.nn.sigmoid(gate_gdn) * y_a + jax.nn.sigmoid(gate_ml) * y_b
    return y.astype(dt) @ w_out

def moe_ffn(h, w_router, b_router, w_gate_up, b_gate_up, w_down, b_down):
    b, s, d = h.shape
    n_tok = b * s
    hf = h.reshape(n_tok, d)
    logits = (hf @ w_router + b_router).astype(jnp.float32)
    top_val, top_idx = lax.top_k(logits, TOP_K)
    gates = jax.nn.softmax(top_val, axis=-1)

    n_assign = n_tok * TOP_K
    n_blocks = -(-n_assign // EXPERT_BLOCK) + N_EXPERTS
    n_rows = n_blocks * EXPERT_BLOCK
    e_flat = top_idx.reshape(-1)
    tok_flat = jnp.repeat(jnp.arange(n_tok, dtype=jnp.int32), TOP_K)
    g_flat = gates.reshape(-1)
    order = jnp.argsort(e_flat)
    e_sorted = e_flat[order]
    counts = jnp.bincount(e_flat, length=N_EXPERTS)
    start = jnp.cumsum(counts) - counts
    padded = (counts + EXPERT_BLOCK - 1) // EXPERT_BLOCK * EXPERT_BLOCK
    pend = jnp.cumsum(padded)
    pstart = pend - padded
    rows = pstart[e_sorted] + (jnp.arange(n_assign) - start[e_sorted])
    row_tok = jnp.zeros((n_rows,), jnp.int32).at[rows].set(tok_flat[order])
    row_gate = jnp.zeros((n_rows,), h.dtype).at[rows].set(g_flat[order].astype(h.dtype))
    block_expert = jnp.minimum(
        jnp.searchsorted(pend, jnp.arange(n_blocks) * EXPERT_BLOCK, side="right"), N_EXPERTS - 1)

    def expert_block(args):
        toks, e = args
        xb = hf[toks]
        gu = xb @ w_gate_up[e] + b_gate_up[e]
        gate = jnp.minimum(gu[..., ::2], SWIGLU_LIMIT)
        up = jnp.clip(gu[..., 1::2], -SWIGLU_LIMIT, SWIGLU_LIMIT)
        act = gate * jax.nn.sigmoid(SWIGLU_ALPHA * gate) * (up + 1.0)
        return act @ w_down[e] + b_down[e]

    y_rows = lax.map(expert_block, (row_tok.reshape(n_blocks, EXPERT_BLOCK), block_expert))
    y_rows = y_rows.reshape(n_rows, d) * row_gate[:, None]
    out = jax.ops.segment_sum(y_rows, row_tok, num_segments=n_tok)
    return out.reshape(b, s, d).astype(h.dtype)

def setup_inputs(seed: int = 0) -> dict:
    key = jax.random.key(seed)
    ks = jax.random.split(key, 24)
    f32 = jnp.float32
    L = DEPTH

    def nrm(k, shape, scale):
        return jax.random.normal(k, shape, f32) * scale

    x = nrm(ks[0], (BATCH, SEQ, D_MODEL), 1.0)
    norm_mix = 1.0 + nrm(ks[1], (L, D_MODEL), 0.02)
    w_in = nrm(ks[2], (L, D_MODEL, D_IN), D_MODEL ** -0.5)
    gdn_conv = nrm(ks[3], (L, CONV_WIDTH, 2 * GDN_QK + GDN_V), CONV_WIDTH ** -0.5)
    gdn_a_log = jnp.log(jax.random.uniform(ks[4], (L, GDN_HEADS), f32, 1.0, 16.0))
    dt = jnp.exp(jax.random.uniform(ks[5], (L, GDN_HEADS), f32, float(np.log(1e-3)),
                                    float(np.log(1e-1))))
    gdn_dt_bias = dt + jnp.log(-jnp.expm1(-dt))
    gdn_norm = 1.0 + nrm(ks[6], (L, GDN_DV), 0.02)
    ml_conv = nrm(ks[7], (L, CONV_WIDTH, 2 * ML_QK), CONV_WIDTH ** -0.5)
    ml_b_i = nrm(ks[8], (L, ML_HEADS), 0.1)
    ml_b_f = jnp.linspace(3.0, 6.0, ML_HEADS, dtype=f32)[None, :] + nrm(ks[9], (L, ML_HEADS), 0.1)
    ml_norm = 1.0 + nrm(ks[10], (L, ML_V), 0.02)
    w_up_gdn = nrm(ks[11], (L, GDN_V, D_MODEL), GDN_V ** -0.5)
    w_up_ml = nrm(ks[12], (L, ML_V, D_MODEL), ML_V ** -0.5)
    w_out = nrm(ks[13], (L, D_MODEL, D_MODEL), D_MODEL ** -0.5)
    norm_ffn = 1.0 + nrm(ks[14], (L, D_MODEL), 0.02)
    w_router = nrm(ks[15], (L, D_MODEL, N_EXPERTS), D_MODEL ** -0.5)
    b_router = nrm(ks[16], (L, N_EXPERTS), 0.01)
    w_gate_up = nrm(ks[17], (L, N_EXPERTS, D_MODEL, 2 * D_EXPERT), D_MODEL ** -0.5)
    b_gate_up = nrm(ks[18], (L, N_EXPERTS, 2 * D_EXPERT), 0.01)
    w_down = nrm(ks[19], (L, N_EXPERTS, D_EXPERT, D_MODEL), D_EXPERT ** -0.5)
    b_down = nrm(ks[20], (L, N_EXPERTS, D_MODEL), 0.01)
    norm_final = 1.0 + nrm(ks[21], (D_MODEL,), 0.02)
    return {"x": x, "norm_mix": norm_mix, "w_in": w_in, "gdn_conv": gdn_conv,
            "gdn_a_log": gdn_a_log, "gdn_dt_bias": gdn_dt_bias, "gdn_norm": gdn_norm,
            "ml_conv": ml_conv, "ml_b_i": ml_b_i, "ml_b_f": ml_b_f, "ml_norm": ml_norm,
            "w_up_gdn": w_up_gdn, "w_up_ml": w_up_ml, "w_out": w_out, "norm_ffn": norm_ffn,
            "w_router": w_router, "b_router": b_router, "w_gate_up": w_gate_up,
            "b_gate_up": b_gate_up, "w_down": w_down, "b_down": b_down,
            "norm_final": norm_final}

def reference(x, norm_mix, w_in, gdn_conv, gdn_a_log, gdn_dt_bias, gdn_norm, ml_conv, ml_b_i,
              ml_b_f, ml_norm, w_up_gdn, w_up_ml, w_out, norm_ffn, w_router, b_router,
              w_gate_up, b_gate_up, w_down, b_down, norm_final):
    for l in range(DEPTH):
        h = rms_norm(x, norm_mix[l])
        x = x + token_mixer(h, w_in[l], gdn_conv[l], gdn_a_log[l], gdn_dt_bias[l], gdn_norm[l],
                            ml_conv[l], ml_b_i[l], ml_b_f[l], ml_norm[l], w_up_gdn[l],
                            w_up_ml[l], w_out[l])
        h = rms_norm(x, norm_ffn[l])
        x = x + moe_ffn(h, w_router[l], b_router[l], w_gate_up[l], b_gate_up[l], w_down[l],
                        b_down[l])
    return rms_norm(x, norm_final)


_drawn_inputs = setup_inputs


def setup_inputs(seed=0):
    import zlib

    import numpy as np

    out = dict(_drawn_inputs(seed))
    spreads = {}
    factors = {'gdn_norm': 2.796,
     'ml_b_i': 32.963,
     'ml_norm': 2.922,
     'b_gate_up': 8.0,
     'b_down': 8.0,
     'norm_final': 7.516}
    for name, (base, spread) in spreads.items():
        noise = np.random.default_rng([zlib.crc32(name.encode()), seed]).standard_normal(out[name].shape)
        drawn = base * np.exp(spread * noise) if base else spread * noise
        out[name] = __import__('jax').numpy.asarray(drawn.astype(out[name].dtype))
    for name, factor in factors.items():
        out[name] = (out[name] * factor).astype(out[name].dtype)
    return out
```

```python
from contextlib import ExitStack

import concourse.bass as bass
from concourse import mybir

F32 = mybir.dt.float32
I32 = mybir.dt.int32
U32 = mybir.dt.uint32
ALU = mybir.AluOpType
ACT = mybir.ActivationFunctionType
AX = mybir.AxisListType

P = 128
GATE_SOFTCAP = 15.0
SWIGLU_LIMIT = 7.0
SWIGLU_ALPHA = 1.702
TOP_K = 4
NORM_EPS = 1e-6
HALF = 512
SLOTS = 64
RING = 8
PIECE = 2048
TAPS = 4


def decoder_layer(nc, x, norm_mix, w_in, gdn_conv, gdn_a_log, gdn_dt_bias, gdn_norm, ml_conv,
                  ml_b_i, ml_b_f, ml_norm, w_up_gdn, w_up_ml, w_out, norm_ffn, w_router,
                  b_router, w_gate_up, b_gate_up, w_down, b_down, norm_final, out):
    _, S, D = x.shape
    E = w_router.shape[2]
    FE = w_down.shape[2]
    H = gdn_a_log.shape[1]
    DH = gdn_norm.shape[1]
    T = S // P
    KC = D // P
    HC = H * DH // P
    assert DH == P and T == 2 and D == 1024 and FE == D and H == 4 and E == 32
    PAIRS = E // 2
    ROUNDS = S // SLOTS
    QS = float(DH) ** -0.5

    width = H * DH
    c_gq, c_gk, c_gv, c_gz = 0, width, 2 * width, 3 * width
    c_ga = 4 * width
    c_gb = c_ga + H
    c_mq = c_gb + H
    c_mk, c_mv, c_mo = c_mq + width, c_mq + 2 * width, c_mq + 3 * width
    c_mi = c_mq + 4 * width
    c_gg = c_mi + 2 * H
    c_gm = c_gg + D
    PW = PIECE // KC
    in_cols = [c + PW * i for c, n in ((c_gq, 2), (c_gk, 2), (c_mq, 2), (c_mk, 2), (c_gv, 2), (c_mv, 2),
                                       (c_gz, 2), (c_mo, 2), (c_gg, 4), (c_gm, 4)) for i in range(n)]
    N_IN = len(in_cols)
    CONV_PIECES, NAT_FIRST, GATE_FIRST = 10, 10, 16
    UP_FIRST = N_IN
    OUT_FIRST = UP_FIRST + 4
    MOE_FIRST = OUT_FIRST + 4
    PER_PAIR = 24
    assert MOE_FIRST % RING == 0 and PER_PAIR % RING == 0

    with ExitStack() as ctx:
        def sb(name, shape, dt=F32):
            return ctx.enter_context(nc.sbuf_tensor(name, shape, dt))

        sems = {}

        def sem(name):
            if name not in sems:
                sems[name] = ctx.enter_context(nc.semaphore(name))
            return sems[name]

        ring = sb("ring", [P, RING, PIECE])
        xs = sb("xs", [P, T, D])
        hn = sb("hn", [P, T, D])
        hT = sb("hT", [P, KC, S])
        cvg = sb("cvg", [P, 3 * HC, S])
        cvm = sb("cvm", [P, 2 * HC, S])
        gate_g = sb("gate_g", [P, KC, S])
        gate_m = sb("gate_m", [P, KC, S])
        z_s = sb("z_s", [P, T, width])
        mo_s = sb("mo_s", [P, T, width])
        mv_s = sb("mv_s", [P, T, width])
        decay = sb("decay", [P, H, T, P])
        pt = sb("pt", [P, H, 3, P])
        lt = sb("lt", [P, H, T, P])
        ltm = sb("ltm", [P, H, T, P])
        inv = sb("inv", [P, H, T, P])
        invT = sb("invT", [P, H, T, P])
        t1 = sb("t1", [P, H, T, P])
        attn = sb("attn", [P, H, T, P])
        vb = sb("vb", [P, H, T, P])
        kd0 = sb("kd0", [P, H, P])
        ua = lt[:, 0:2, :, :].rearrange("p h t i -> p (h t) i")
        ub = lt[:, 2:4, :, :].rearrange("p h t i -> p (h t) i")
        st = ltm[:, 0:2, :, :].rearrange("p h t i -> p (h t) i")
        om = hn[:, 0, :].rearrange("p (t c) -> p t c", t=T)
        og = hn[:, 1, :].rearrange("p (t c) -> p t c", t=T)
        scr = cvm[:, 2 * HC - 2:2 * HC, :].rearrange("p a s -> p (a s)")
        ident = sb("ident", [P, P])
        triu = sb("triu", [P, P])
        striu = sb("striu", [P, P])
        ones = sb("ones", [P, P])
        LEVELS = [1 << s for s in range(7)]
        level = sb("level", [P, len(LEVELS), P])
        prm = sb("prm", [96, P])
        prmT = sb("prmT", [P, 96])
        wsc = sb("wsc", [P, KC, 4 * H])
        sbias = sb("sbias", [P, 4 * H])
        alog = sb("alog", [P, H])
        gnorm = sb("gnorm", [P, DH])
        mnorm = sb("mnorm", [P, width])
        fnorm = sb("fnorm", [P, D])
        brt = sb("brt", [P, E])
        wr = sb("wr", [P, KC, E])
        bgu = sb("bgu", [P, 2 * FE])
        pre = sb("pre", [P, T, 4 * H])
        th = sb("th", [P, T, 2 * H])
        q8 = sb("q8", [P, T, 2 * H])
        a8 = sb("a8", [P, T, 2 * H])
        e8 = sb("e8", [P, T, 2 * H])
        g8 = sb("g8", [P, T, 2 * H])
        rowsrc = sb("rowsrc", [P, T, 2 * H])
        fcum = sb("fcum", [P, T, H])
        acol = sb("acol", [P, T, H])
        ex8 = sb("ex8", [P, 2 * H])
        rows = sb("rows", [2 * H, S])
        arow = sb("arow", [H, S])
        cmrow = sb("cmrow", [H, S])
        dmin = sb("dmin", [P, T, H])
        den = sb("den", [P, T, H])
        ss = sb("ss", [P, 2 * H])
        rstd = sb("rstd", [P, 2 * H])
        lg = sb("lg", [P, T, E])
        mx8 = sb("mx8", [P, T, 8])
        ix8 = sb("ix8", [P, T, 8], U32)
        ixf = sb("ixf", [P, T, 8])
        g4 = sb("g4", [P, T, TOP_K])
        gsum = sb("gsum", [P, T])
        eiota = sb("eiota", [P, E])
        siota = sb("siota", [P, SLOTS])
        eq = sb("eq", [P, TOP_K, E])
        chosen = sb("chosen", [P, T, E])
        gates = sb("gates", [P, T, E])
        gatesT = sb("gatesT", [E, S])
        cnt = sb("cnt", [P, 4])
        n_pairs = sb("n_pairs", [P, 1], I32)
        XCOLS = ROUNDS * E + 2
        posx = sb("posx", [P, T, XCOLS])
        gatex = sb("gatex", [P, T, XCOLS])
        pick = sb("pick", [P, XCOLS])

        bank = [ctx.enter_context(nc.psum_tensor(f"bank{i}", [P, HALF], F32)) for i in range(4)]
        bank45 = ctx.enter_context(nc.psum_tensor("bank45", [P, 2, HALF], F32))
        bank67 = ctx.enter_context(nc.psum_tensor("bank67", [P, 2, HALF], F32))
        B = [b[:, :] for b in bank] + [bank45[:, 0, :], bank45[:, 1, :], bank67[:, 0, :], bank67[:, 1, :]]

        onehot = decay[:, 0, :, :]
        weighted = decay[:, 1, :, :]
        scat = decay[:, 2, :, :]
        picked = decay[:, 3, :, :].rearrange("p t (a s) -> p t a s", a=2)[:, 0, :, :]
        xT = cvg[:, 0:4, :].rearrange("p a (b s) -> p (a b) s", b=2)
        act = cvg[:, 4:8, :].rearrange("p (e a) s -> p e (a s)", e=2)
        actT = cvg[:, 8:12, :].rearrange("p (e a) s -> p e (a s)", e=2)
        glu_g = cvm[:, 0:2, :].rearrange("p a s -> p (a s)")
        glu_u = cvm[:, 2:4, :].rearrange("p a s -> p (a s)")
        glu_s = cvm[:, 4:6, :].rearrange("p a s -> p (a s)")
        ysb = vb[:, :, :, :].rearrange("p h t i -> p (h t i)")

        bdn = gate_m[0:E, KC // 2:KC, :].rearrange("p a s -> p (a s)")
        eq_rows = gate_m[0:E, 0, :]

        def landed(eng, j):
            eng.wait_ge(sem(f"ring_full{j % RING if isinstance(j, int) else 0}"), 16 * (j // RING + 1))

        def landed_in_pair(eng, n, local):
            first = (MOE_FIRST + 2 * 8 - PER_PAIR) // RING
            eng.wait_ge(sem(f"ring_full{local % RING}"), (n * (PER_PAIR // RING) + (first + local // RING + 1)) * 16)

        def pieces_before(n, local):
            return n * PER_PAIR + (MOE_FIRST + 2 * 8 - PER_PAIR + local)

        w_in_v = w_in.rearrange("l (k p) c -> p (l k) c", p=P)
        up_v = [w.rearrange("l (k p) c -> p (l k) c", p=P) for w in (w_up_ml, w_up_gdn)]
        out_v = w_out.rearrange("l (k p) c -> p (l k) c", p=P)
        gu_v = w_gate_up.rearrange("l e (k p) c -> (l e) p k c", p=P)
        dn_v = w_down.rearrange("l e (k p) c -> (l e) p k c", p=P)

        def slot3(j, k):
            return ring[:, j % RING, :].rearrange("p (k c) -> p k c", k=k)

        block = ctx.enter_context(nc.Block())

        @block.sync
        def _(sp):
            sp.dma_start(xs[:, :, :], x.rearrange("b (t p) d -> p (b t) d", p=P)).then_inc(sem("x_loaded"), 16)

            def put(j, local, src, k):
                sp.dma_start(slot3(local, k), src).then_inc(sem(f"ring_full{local % RING}"), 16)

            for j in range(MOE_FIRST):
                if j >= RING:
                    sp.wait_ge(sem("piece_done"), j - RING + 1)
                if j < N_IN:
                    put(j, j, w_in_v[:, :, in_cols[j]:in_cols[j] + PW], KC)
                elif j < OUT_FIRST:
                    i = j - UP_FIRST
                    put(j, j, up_v[i // 2][:, :, (i % 2) * HALF:(i % 2 + 1) * HALF], HC)
                else:
                    i = j - OUT_FIRST
                    put(j, j, out_v[:, 2 * i:2 * i + 2, :], 2)

            def gate_up(e, local, used):
                for k in range(KC):
                    sp.wait_ge(sem("piece_done"), used(local + k))
                    put(None, local + k, gu_v[bass.ds(e, 1), :, k, :].rearrange("e p c -> p e c"), 1)

            def down(e0, local, used):
                for i in range(8):
                    sp.wait_ge(sem("piece_done"), used(local + i))
                    put(None, local + i,
                        dn_v[bass.ds(e0 + i % 2, 1), :, 2 * (i // 2):2 * (i // 2) + 2, :].rearrange("e p k c -> p (e k) c"), 2)

            gate_up(0, 0, lambda l: MOE_FIRST + l - RING + 1)
            gate_up(1, 8, lambda l: MOE_FIRST + l - RING + 1)

            def pair(n, p, before):
                used = lambda l: pieces_before(n, l) - RING + 1
                gate_up(p * 2, 0, used)
                down(before * 2, 8, used)
                gate_up(p * 2 + 1, 16, used)

            with sp.Fori(1, PAIRS) as n:
                pair(n, n, n - 1)
            sp.wait_ge(sem("n_pairs_ready"), 1)
            last = sp.value_load(n_pairs[0:1, 0:1], min_val=PAIRS, max_val=PAIRS * ROUNDS)
            with sp.If(last > PAIRS):
                with sp.Fori(PAIRS, last) as n:
                    pair(n, n % PAIRS, (n - 1) % PAIRS)
            down(2 * (PAIRS - 1), 0, lambda l: pieces_before(last, l) - RING + 1)
            sp.wait_ge(sem("result_ready"), T)
            sp.dma_start(out.rearrange("b (t p) d -> p (b t) d", p=P), hn[:, :, :]).then_inc(sem("stored"), 16)
            sp.wait_ge(sem("stored"), 16)

        @block.gpsimd
        def _(pool):
            n = [0]

            def link(ins):
                n[0] += 1
                ins.then_inc(sem("pool_step"), 1)
                pool.wait_ge(sem("pool_step"), n[0])

            link(pool.memset(ident[:, :], 0.0))
            pool.affine_select(out=ident[:, :], in_=ident[:, :], compare_op=ALU.not_equal, fill=1.0, base=0,
                               pattern=[[-1, P]], channel_multiplier=1).then_inc(sem("ident_ready"), 1)
            link(pool.memset(ones[:, :], 1.0))
            pool.affine_select(out=triu[:, :], in_=ones[:, :], compare_op=ALU.is_ge, fill=0.0, base=0,
                               pattern=[[1, P]], channel_multiplier=-1).then_inc(sem("masks_ready"), 1)
            pool.affine_select(out=striu[:, :], in_=ones[:, :], compare_op=ALU.is_ge, fill=0.0, base=-1,
                               pattern=[[1, P]], channel_multiplier=-1).then_inc(sem("masks_ready"), 1)
            link(pool.memset(level[:, :, :], 0.0))
            for m, s in enumerate(LEVELS):
                v = level[:, m, :].rearrange("p (b h r) -> p b h r", h=2, r=s)[:, :, 1, :]
                link(pool.memset(v, -1.0))
                link(pool.affine_select(out=v, in_=v, compare_op=ALU.is_ge, fill=0.0, base=0,
                                        pattern=[[-2 * s, P // (2 * s)], [0, s]], channel_multiplier=1))
                pool.affine_select(out=v, in_=v, compare_op=ALU.is_ge, fill=0.0, base=s - 1,
                                   pattern=[[2 * s, P // (2 * s)], [0, s]],
                                   channel_multiplier=-1).then_inc(sem("levels_ready"), 1)
            pool.iota(eiota[:, :], [[1, E]], base=0, channel_multiplier=0,
                      allow_small_or_imprecise_dtypes=True).then_inc(sem("tables_ready"), 1)
            pool.iota(siota[:, :], [[1, SLOTS]], base=0, channel_multiplier=0,
                      allow_small_or_imprecise_dtypes=True).then_inc(sem("tables_ready"), 1)
            pool.wait_ge(sem("ident_ready"), 1)
            for r in range(ROUNDS):
                pool.tensor_copy(pick[:, r * E:(r + 1) * E], ident[:, 0:E]).then_inc(sem("tables_ready"), 1)
            pool.memset(pick[:, ROUNDS * E:], 0.0).then_inc(sem("tables_ready"), 1)
            link(pool.memset(bgu[:, :], 0.0))
            pool.memset(prmT[:, 0:1], 0.0).then_inc(sem("bgu_zeroed"), 1)

        TABLES = 2 + ROUNDS + 1

        @block.tensor
        def _(pe):
            def proj(j):
                dst = B[6 + j % 2]
                landed(pe, j)
                if 2 <= j <= CONV_PIECES + 1:
                    pe.wait_ge(sem("conv_done"), 2 * (j - 1))
                if j >= CONV_PIECES + 2:
                    pe.wait_ge(sem("proj_taken"), j - 1 - CONV_PIECES)
                w = slot3(j, KC)
                for c in range(2):
                    for k in range(KC):
                        if NAT_FIRST <= j < GATE_FIRST:
                            lhs, rhs = hT[:, k, c * P:(c + 1) * P], w[:, k, :]
                        else:
                            lhs, rhs = w[:, k, c * P:(c + 1) * P], hT[:, k, :]
                        mm = pe.matmul(dst[:, c * S:(c + 1) * S], lhs, rhs, start=(k == 0), stop=(k == KC - 1))
                mm.then_inc(sem("piece_done"), 1)

            def transposes(src, banks, signal):
                for i, s in enumerate(src):
                    mm = pe.transpose(B[banks[i // 4]][:, (i % 4) * P:(i % 4 + 1) * P], s, ident[:, :])
                    if i % 4 == 3 or i == len(src) - 1:
                        mm.then_inc(sem(signal), 1)

            def per_head(banks, signal, product):
                for h in range(H):
                    for t in range(T):
                        i = h * T + t
                        lhs, rhs = product(h, t)
                        mm = pe.matmul(B[banks[i // 4]][:, (i % 4) * P:(i % 4 + 1) * P], lhs, rhs, start=True, stop=True)
                        if i % 4 == 3:
                            mm.then_inc(sem(signal), 1)

            def chunk_products(bnk, signal, product):
                for h in range(H):
                    lhs, rhs = product(h)
                    mm = pe.matmul(B[bnk][:, h * P:(h + 1) * P], lhs, rhs, start=True, stop=True)
                mm.then_inc(sem(signal), 1)

            pe.wait_ge(sem("ident_ready"), 1)
            pe.wait_ge(sem("prm_loaded"), 64)
            pe.transpose(B[4][:, 0:96], prm[:, :], ident[0:96, 0:96]).then_inc(sem("prm_turned"), 1)
            for t in range(T):
                pe.wait_ge(sem("hn_ready"), t + 1)
                transposes([hn[:, t, k * P:(k + 1) * P] for k in range(KC)], [2 * t, 2 * t + 1], "h_turned")
            pe.wait_ge(sem("scal_loaded"), 32)
            pe.wait_ge(sem("hT_ready"), 2 * T)
            for t in range(T):
                for k in range(KC):
                    mm = pe.matmul(B[5][:, t * 4 * H:(t + 1) * 4 * H], hT[:, k, t * P:(t + 1) * P], wsc[:, k, :],
                                   start=(k == 0), stop=(k == KC - 1))
            mm.then_inc(sem("scal_done"), 1)
            proj(0)
            proj(1)
            pe.wait_ge(sem("masks_ready"), 2)
            pe.wait_ge(sem("log_decay_ready"), 2)
            pe.matmul(B[5][:, 64:64 + 2 * H], triu[:, :], g8[:, 0, :], start=True, stop=True)
            pe.matmul(B[5][:, 64 + 2 * H:64 + 4 * H], triu[:, :], g8[:, 1, :], start=True, stop=False,
                      skip_group_check=True)
            pe.matmul(B[5][:, 64 + 3 * H:64 + 4 * H], ones[:, :], g8[:, 0, H:2 * H], start=False, stop=True,
                      skip_group_check=True)
            pe.matmul(B[5][:, 96:96 + H], ones[:, :], g8[:, 0, 0:H], start=True, stop=True,
                      skip_group_check=True).then_inc(sem("cum_done"), 1)
            proj(2)
            pe.wait_ge(sem("row_source_ready"), 1)
            for t in range(T):
                pe.transpose(B[5][0:2 * H, 128 + t * P:128 + (t + 1) * P], rowsrc[:, t, :], ident[:, :])
            for t in range(T):
                mm = pe.transpose(B[4][0:H, 128 + t * P:128 + (t + 1) * P], acol[:, t, :], ident[:, :])
            mm.then_inc(sem("rows_turned"), 1)
            proj(3)
            pe.wait_ge(sem("squares_ready"), 1)
            for i in range(HC):
                mm = pe.matmul(B[2 + i // 2][:, (i % 2) * S:(i % 2 + 1) * S], ones[:, :], attn[:, i, :, :],
                               start=True, stop=True)
            mm.then_inc(sem("norm_sums"), 1)
            pe.wait_ge(sem("rows_ready"), 1)
            for t in range(T):
                mm = pe.transpose(B[5][:, 480 + t * H:480 + (t + 1) * H], cmrow[:, t * P:(t + 1) * P], ident[0:H, 0:H])
            mm.then_inc(sem("runmax_turned"), 1)

            def spread(src, first, banks, signal):
                n = src.shape[0]
                for h in range(H):
                    mm = pe.matmul(B[banks[h // 2]][:, (h % 2) * S:(h % 2 + 1) * S],
                                   ident[0:n, first + h:first + h + 1].to_broadcast([n, P]), src[:, :],
                                   start=True, stop=True)
                mm.then_inc(sem(signal), 1)

            pe.wait_ge(sem("hT_ready"), 2 * T)
            spread(rows, 0, (0, 1), "decay_spread")
            proj(4)
            pe.wait_ge(sem("squares_ready"), 2)
            pe.wait_ge(sem("roots_ready"), 1)
            for i in range(HC):
                mm = pe.matmul(B[2 + i // 2][:, (i % 2) * S:(i % 2 + 1) * S], ones[:, :], attn[:, i, :, :],
                               start=True, stop=True)
            mm.then_inc(sem("norm_sums"), 1)
            proj(5)
            pe.wait_ge(sem("roots_ready"), 2)
            spread(rows, H, (2, 3), "beta_spread")
            pe.wait_ge(sem("dmin_ready"), 1)
            spread(cmrow, 0, (4, 5), "runmax_spread")
            proj(6)
            pe.wait_ge(sem("k_normed"), 1)
            pe.wait_ge(sem("decay_ready"), 1)
            kT = lambda h, t: cvg[:, HC + h, t * P:(t + 1) * P]
            qT = lambda h, t: cvg[:, h, t * P:(t + 1) * P]
            per_head((0, 1), "kk_done", lambda h, t: (kT(h, t), kT(h, t)))
            proj(7)
            pe.wait_ge(sem("q_normed"), 1)
            pe.wait_ge(sem("pt_log_ready"), 1)
            per_head((4, 5), "kq_done", lambda h, t: (kT(h, t), qT(h, t)))
            proj(8)
            def level_t1(m):
                pe.wait_ge(sem("level_ready"), m + 1)
                per_head((0, 1), "t1_done",
                         lambda h, t: (ltm[:, h, t, :], ident[:, :] if m == 0 else inv[:, h, t, :]))

            def level_pq(m):
                pe.wait_ge(sem("t1_ready"), m)
                if m < len(LEVELS) - 1:
                    per_head((2, 3), "p_done", lambda h, t: (invT[:, h, t, :], t1[:, h, t, :]))
                per_head((4, 5), "q_done", lambda h, t: (t1[:, h, t, :], invT[:, h, t, :]))

            level_t1(0)
            proj(9)
            pe.wait_ge(sem("mlstm_qk_ready"), 1)
            pe.wait_ge(sem("attn_ready"), 1)
            pe.wait_ge(sem("level_ready"), 1)
            for h in range(H):
                pe.matmul(B[2 + h][:, 0:S], cvm[:, HC + h, 0:P], cvm[:, h, :], start=True, stop=True)
                pe.matmul(B[2 + h][:, S:S + P], cvm[:, HC + h, P:S], cvm[:, h, P:S], start=True,
                          stop=True).then_inc(sem("ml_kq_done"), 1)
            proj(10)
            level_t1(1)
            proj(11)
            pe.wait_ge(sem("pt_ready"), H)
            level_pq(1)
            pe.wait_ge(sem("conv_silu"), 3 * HC + 2 * HC)
            transposes([cvg[:, 2 * HC + h, t * P:(t + 1) * P] for h in range(H) for t in range(T)], (0, 1), "v_turned")
            proj(12)
            pe.wait_ge(sem("vb_ready"), 1)
            level_t1(2)
            proj(13)
            level_pq(2)
            transposes([kT(h, 0) for h in range(H)], (0,), "k_turned")
            proj(14)
            pe.wait_ge(sem("kd_ready"), 1)
            level_t1(3)
            proj(15)
            level_pq(3)
            proj(16)
            level_t1(4)
            pe.wait_ge(sem("proj_taken"), 2)
            pe.wait_ge(sem("inv_ready"), 3)
            for t in range(T):
                for h in range(H):
                    for j in range(t + 1):
                        w = pt[:, h, t + j, :]
                        pe.matmul(B[2 + t][:, h * P:(h + 1) * P], w, mv_s[:, j, h * DH:(h + 1) * DH],
                                  start=(j == 0), stop=(j == t))
            for t in range(T):
                for h in range(H):
                    for j in range(t + 1):
                        mm = pe.matmul(B[4][:, t * H + h:t * H + h + 1], pt[:, h, t + j, :], ones[:, 0:1],
                                       start=(j == 0), stop=(j == t))
            mm.then_inc(sem("ml_sums_done"), 1)
            proj(17)
            pe.wait_ge(sem("ml_sums_taken"), 1)
            level_pq(4)
            proj(18)
            level_t1(5)
            proj(19)
            level_pq(5)
            proj(20)
            level_t1(6)
            proj(21)
            level_pq(6)
            pe.wait_ge(sem("om_ready"), 1)
            pe.wait_ge(sem("inv_ready"), 5)
            transposes([om[:, t, h * P:(h + 1) * P] for h in range(H) for t in range(T)], (2, 3), "om_turned")
            proj(22)
            pe.wait_ge(sem("inv_ready"), 6)
            chunk_products(0, "u0_done", lambda h: (invT[:, h, 0, :], vb[:, h, 0, :]))
            proj(23)
            pe.wait_ge(sem("u0_ready"), 1)
            chunk_products(1, "state_done", lambda h: (kd0[:, h, :], ua[:, h, :]))
            chunk_products(4, "o0_done", lambda h: (attn[:, h, 0, :], ua[:, h, :]))

            def lift(i):
                j = UP_FIRST + i
                landed(pe, j)
                if i == 0:
                    pe.wait_ge(sem("proj_taken"), N_IN - CONV_PIECES)
                if i >= 1:
                    pe.wait_ge(sem("lift_taken"), i)
                src = cvm[:, 0:HC, :] if i < 2 else cvg[:, 2 * HC:3 * HC, :]
                w = slot3(j, HC)
                for c in range(4):
                    for k in range(HC):
                        mm = pe.matmul(B[6 + c // 2][:, (c % 2) * S:(c % 2 + 1) * S], w[:, k, c * P:(c + 1) * P],
                                       src[:, k, :], start=(k == 0), stop=(k == HC - 1))
                mm.then_inc(sem("piece_done"), 1)

            pe.wait_ge(sem("omT_ready"), 1)
            lift(0)
            pe.wait_ge(sem("state_ready"), 1)
            chunk_products(0, "ks_done", lambda h: (kT(h, 1), st[:, h, :]))
            chunk_products(1, "qs_done", lambda h: (qT(h, 1), st[:, h, :]))
            lift(1)
            pe.wait_ge(sem("rhs1_ready"), 1)
            chunk_products(0, "u1_done", lambda h: (invT[:, h, 1, :], ub[:, h, :]))
            pe.wait_ge(sem("u1_ready"), 1)
            pe.wait_ge(sem("omT_ready"), 1)
            chunk_products(2, "au_done", lambda h: (attn[:, h, 1, :], ua[:, h, :]))
            pe.wait_ge(sem("og_ready"), 1)
            transposes([og[:, t, h * P:(h + 1) * P] for h in range(H) for t in range(T)], (4, 5), "og_turned")
            pe.wait_ge(sem("ogT_ready"), 1)
            lift(2)
            lift(3)
            pe.wait_ge(sem("lift_taken"), 4)
            for i in range(4):
                j = OUT_FIRST + i
                landed(pe, j)
                w = slot3(j, 2)
                for k in range(2):
                    for t in range(T):
                        for n in range(2):
                            kk = 2 * i + k
                            mm = pe.matmul(B[2 * t + n], gate_g[:, kk, t * P:(t + 1) * P], w[:, k, n * HALF:(n + 1) * HALF],
                                           start=(kk == 0), stop=(kk == KC - 1))
                mm.then_inc(sem("piece_done"), 1)
            for t in range(T):
                pe.wait_ge(sem("h2_ready"), t + 1)
                transposes([hn[:, t, k * P:(k + 1) * P] for k in range(KC)], [4 + 2 * t, 5 + 2 * t], "h2_turned")
            pe.wait_ge(sem("h2T_ready"), 2 * T)
            pe.wait_ge(sem("tail_params"), 16 * 5)
            for k in range(KC):
                mm = pe.matmul(B[0][0:E, 0:S], wr[:, k, :], hT[:, k, :], start=(k == 0), stop=(k == KC - 1))
            mm.then_inc(sem("logitsT_done"), 1)
            pe.wait_ge(sem("logitsT_ready"), 1)
            for t in range(T):
                mm = pe.transpose(B[1][:, t * E:(t + 1) * E], eq_rows[:, t * P:(t + 1) * P], ident[0:E, 0:E])
            mm.then_inc(sem("logits_done"), 1)
            pe.wait_ge(sem("chosen_ready"), 1)
            pe.matmul(B[4][:, 0:E], striu[:, :], chosen[:, 0, :], start=True, stop=True)
            pe.matmul(B[4][:, E:2 * E], striu[:, :], chosen[:, 1, :], start=True, stop=False)
            pe.matmul(B[4][:, E:2 * E], ones[:, :], chosen[:, 0, :], start=False, stop=True)
            pe.matmul(B[4][:, 2 * E:3 * E], ones[:, :], chosen[:, 0, :], start=True, stop=False)
            pe.matmul(B[4][:, 2 * E:3 * E], ones[:, :], chosen[:, 1, :], start=False,
                      stop=True).then_inc(sem("ranks_done"), 1)
            pe.wait_ge(sem("gates_ready"), 1)
            for t in range(T):
                mm = pe.transpose(B[5][0:E, t * P:(t + 1) * P], gates[:, t, :], ident[:, :])
            mm.then_inc(sem("gates_turned"), 1)

            def gather(n):
                pe.wait_ge(sem("onehot_ready"), 2 * T * (n + 1) if isinstance(n, int) else n * (2 * T) + 2 * T)
                for b in range(2):
                    if isinstance(n, int):
                        pe.wait_ge(sem("h2T_ready"), 2 * T)
                    elif b == 0:
                        pe.wait_ge(sem("turned_copied"), n * 2 - 1)
                    for k in range(KC // 2 * b, KC // 2 * (b + 1)):
                        for t in range(T):
                            mm = pe.matmul(B[6 + b][:, (k % 4) * P:(k % 4 + 1) * P], hn[:, t, k * P:(k + 1) * P],
                                           onehot[:, t, :], start=(t == 0), stop=(t == T - 1))
                    mm.then_inc(sem("gathered"), 1)

            def gate_up(n, e, local):
                pe.wait_ge(sem("xT_ready"), n * 2 + 2)
                pe.wait_ge(sem("picked_ready"), n * 2 + 2)
                if e == 0:
                    if not isinstance(n, int):
                        pe.wait_ge(sem("gu_taken"), n * 2)
                else:
                    pe.wait_ge(sem("gu_taken"), n * 2 + 1)
                for half in range(2):
                    for side in range(2):
                        at = side * FE + half * HALF
                        pe.matmul(B[4 + half][side * SLOTS:(side + 1) * SLOTS, :], picked[:, e, :], bgu[:, at:at + HALF],
                                  start=True, stop=False, skip_group_check=True)
                for k in range(KC):
                    if isinstance(n, int):
                        landed(pe, MOE_FIRST + local + k)
                    else:
                        landed_in_pair(pe, n, local + k)
                    for half in range(2):
                        for side in range(2):
                            at = side * FE + half * HALF
                            mm = pe.matmul(B[4 + half][side * SLOTS:(side + 1) * SLOTS, :], xT[:, k, e * SLOTS:(e + 1) * SLOTS],
                                           ring[:, (local + k) % RING, at:at + HALF], start=False, stop=(k == KC - 1),
                                           skip_group_check=True)
                    mm.then_inc(sem("piece_done"), 1)

            def down(n, local):
                pe.wait_ge(sem("turned_copied"), n * 2)
                pe.wait_ge(sem("xT_ready"), n * 2)
                for i in range(0, 8, 2):
                    landed_in_pair(pe, n, local + i)
                    landed_in_pair(pe, n, local + i + 1)
                    for k in range(2):
                        block_ = i + k
                        col = (block_ % 4) * P + (block_ // 4) * SLOTS
                        for half in range(2):
                            for e in range(2):
                                mm = pe.matmul(B[6 + half][e * SLOTS:(e + 1) * SLOTS, :], actT[:, e, col:col + SLOTS],
                                               slot3(local + i + e, 2)[:, k, half * HALF:(half + 1) * HALF],
                                               start=(i == 0 and k == 0), stop=(i == 6 and k == 1),
                                               skip_group_check=True)
                                if k == 1 and half == 1:
                                    mm.then_inc(sem("piece_done"), 1)

            def turn_act(n, e):
                pe.wait_ge(sem("act_ready"), n * 2 + (e + 1))
                for c in range(4):
                    mm = pe.transpose(B[6 + e][:, c * P:(c + 1) * P], act[:, e, c * P:(c + 1) * P], ident[:, :])
                mm.then_inc(sem("act_turned"), 1)

            def turn_weighted(n):
                pe.wait_ge(sem("weighted_ready"), n * (2 * T) + 2 * T)
                for t in range(T):
                    mm = pe.transpose(B[6][:, t * P:(t + 1) * P], weighted[:, t, :], ident[:, :])
                mm.then_inc(sem("weighted_turned"), 1)

            def scatter(n):
                pe.wait_ge(sem("y_copied"), n * 2)
                pe.wait_ge(sem("scat_ready"), n)
                for t in range(T):
                    for half in range(2):
                        mm = pe.matmul(B[2 * t + half], scat[:, t, :], ysb[:, half * HALF:(half + 1) * HALF],
                                       start=False, stop=False, skip_group_check=True)
                mm.then_inc(sem("scattered"), 1)

            gather(0)
            pe.wait_ge(sem("gatesT_ready"), 1)
            pe.wait_ge(sem("bdn_loaded"), 16)
            for t in range(T):
                for half in range(2):
                    pe.matmul(B[2 * t + half], gatesT[:, t * P:(t + 1) * P], bdn[:, half * HALF:(half + 1) * HALF],
                              start=True, stop=False, skip_group_check=True)
            pe.wait_ge(sem("expert_bias"), 16)
            pe.wait_ge(sem("n_pairs_ready"), 1)
            last = pe.value_load(n_pairs[0:1, 0:1], min_val=PAIRS, max_val=PAIRS * ROUNDS)
            gate_up(0, 0, 0)
            gate_up(0, 1, 8)
            turn_act(0, 0)
            pe.wait_ge(sem("turned_copied"), 1)

            def next_pair(n):
                pe.wait_ge(sem("onehot_ready"), n * (2 * T) + 4 * T)
                for b in (1, 0):
                    if b == 0:
                        pe.wait_ge(sem("turned_copied"), n * 2 + 1)
                    for k in range(KC // 2 * b, KC // 2 * (b + 1)):
                        for t in range(T):
                            mm = pe.matmul(B[6 + b][:, (k % 4) * P:(k % 4 + 1) * P], hn[:, t, k * P:(k + 1) * P],
                                           onehot[:, t, :], start=(t == 0), stop=(t == T - 1))
                    mm.then_inc(sem("gathered"), 1)
                pe.wait_ge(sem("xT_ready"), n * 2 + 3)
                turn_act(n, 1)
                pe.wait_ge(sem("xT_ready"), n * 2 + 4)
                turn_weighted(n)

            next_pair(0)
            with pe.Fori(1, last) as n:
                gate_up(n, 0, 0)
                pe.wait_ge(sem("scat_ready"), n)
                down(n, 8)
                gate_up(n, 1, 16)
                pe.wait_ge(sem("y_copied"), n * 2)
                turn_act(n, 0)
                scatter(n)
                next_pair(n)
            pe.wait_ge(sem("scat_ready"), last)
            down(last, 0)
            pe.wait_ge(sem("y_copied"), last * 2)
            for t in range(T):
                for half in range(2):
                    mm = pe.matmul(B[2 * t + half], scat[:, t, :], ysb[:, half * HALF:(half + 1) * HALF],
                                   start=False, stop=True, skip_group_check=True)
            mm.then_inc(sem("sums_done"), 1)

        @block.vector
        def _(dve):
            steps = [0]

            def link(ins):
                steps[0] += 1
                ins.then_inc(sem("dve_step"), 1)
                dve.wait_ge(sem("dve_step"), steps[0])

            def signal(ins, name):
                ins.then_inc(sem(name), 1)

            def bc(ap, shape):
                return ap.to_broadcast(shape)

            dve.wait_ge(sem("x_squared"), T)
            link(dve.tensor_scalar(ss[:, 0:T], ss[:, 0:T], 1.0 / D, NORM_EPS, ALU.mult, ALU.add))
            dve.memset(sbias[:, H:2 * H], 0.0).then_inc(sem("ms_ready"), 1)
            dve.wait_ge(sem("root_x"), 1)
            link(dve.reciprocal(rstd[:, 0:T], rstd[:, 0:T]))
            for t in range(T):
                signal(dve.tensor_scalar(hn[:, t, :], xs[:, t, :], rstd[:, t:t + 1], None, ALU.mult), "hn_ready")
            dve.wait_ge(sem("prm_turned"), 1)
            dve.wait_ge(sem("bgu_zeroed"), 1)
            link(dve.tensor_copy(prmT[:, :], B[4][:, 0:96]))
            for b in range(2 * T):
                dve.wait_ge(sem("h_turned"), b + 1)
                t, k = b // 2, 4 * (b % 2)
                signal(dve.tensor_tensor(hT[:, k:k + 4, t * P:(t + 1) * P], B[b].rearrange("p (k i) -> p k i", k=4),
                                         bc(prmT[:, 80 + k:84 + k].unsqueeze(2), [P, 4, P]), ALU.mult), "hT_ready")
            dve.wait_ge(sem("scal_done"), 1)
            dve.wait_ge(sem("sbias_loaded"), 64)
            signal(dve.tensor_tensor(pre[:, :, :], B[5][:, 0:T * 4 * H].rearrange("p (t c) -> p t c", t=T),
                                     bc(sbias[:, :].unsqueeze(1), [P, T, 4 * H]), ALU.add), "pre_ready")
            dve.wait_ge(sem("pre_ready"), 1)
            signal(dve.tensor_copy(q8[:, :, 0:H], pre[:, :, 0:H]), "q8_ready")
            dve.wait_ge(sem("th_ready"), 1)
            signal(dve.tensor_scalar(q8[:, :, H:2 * H], th[:, :, H:2 * H], -GATE_SOFTCAP, None, ALU.mult), "q8_ready")
            dve.wait_ge(sem("q8_ready"), 2)
            dve.scalar_tensor_tensor(out=a8[:, :, :], in0=q8[:, :, :], scalar=-1.0, in1=q8[:, :, :],
                                     op0=ALU.mult, op1=ALU.max).then_inc(sem("a8_ready"), 1)

            conv_n = [0]

            def conv(j):
                for c in range(2):
                    i = 2 * j + c
                    if i < 2 * HC:
                        dst, col, stride = cvg[:, i, :], i, 3 * HC
                    elif i < 4 * HC:
                        dst, col, stride = cvm[:, i - 2 * HC, :], 3 * HC * TAPS + i - 2 * HC, 2 * HC
                    else:
                        dst, col, stride = cvg[:, i - 2 * HC, :], i - 2 * HC, 3 * HC
                    src = B[6 + j % 2][:, c * S:(c + 1) * S]
                    if c == 0:
                        dve.wait_ge(sem("conv_tap3"), 2 * j + 2)
                    for tap in (2, 1, 0):
                        d = TAPS - 1 - tap
                        w = prmT[:, col + tap * stride:col + tap * stride + 1]
                        ins = dve.scalar_tensor_tensor(out=dst[:, d:], in0=src[:, 0:S - d], scalar=w, in1=dst[:, d:],
                                                       op0=ALU.mult, op1=ALU.add)
                        if tap:
                            link(ins)
                        else:
                            ins.then_inc(sem("conv_done"), 1)

            conv(0)
            conv(1)
            dve.wait_ge(sem("softlog_ready"), 1)
            link(dve.scalar_tensor_tensor(out=g8[:, :, :], in0=q8[:, :, :], scalar=0.0, in1=e8[:, :, :],
                                          op0=ALU.max, op1=ALU.add))
            dve.scalar_tensor_tensor(out=g8[:, :, 0:H], in0=g8[:, :, 0:H], scalar=-1.0,
                                     in1=bc(alog[:, :].unsqueeze(1), [P, T, H]), op0=ALU.mult,
                                     op1=ALU.mult).then_inc(sem("log_decay_ready"), 1)
            dve.tensor_scalar(g8[:, :, H:2 * H], g8[:, :, H:2 * H], -1.0, None, ALU.mult).then_inc(sem("log_decay_ready"), 1)
            dve.wait_ge(sem("cum_done"), 1)
            cum = B[5][:, 64:64 + T * 2 * H].rearrange("p (t c) -> p t c", t=T)
            link(dve.tensor_copy(rowsrc[:, :, 0:H], cum[:, :, 0:H]))
            link(dve.tensor_copy(fcum[:, :, :], cum[:, :, H:2 * H]))
            link(dve.scalar_tensor_tensor(out=acol[:, :, :], in0=th[:, :, 0:H], scalar=GATE_SOFTCAP, in1=fcum[:, :, :],
                                          op0=ALU.mult, op1=ALU.subtract))
            link(dve.tensor_tensor(ex8[:, 0:H], B[5][:, 96:96 + H], rowsrc[:, 0, 0:H], ALU.subtract))
            dve.tensor_copy(ex8[:, H:2 * H], rowsrc[:, 1, 0:H]).then_inc(sem("row_source_ready"), 1)
            conv(2)
            dve.wait_ge(sem("rows_turned"), 1)
            link(dve.tensor_copy(rows[:, :], B[5][0:2 * H, 128:128 + S]))
            link(dve.tensor_copy(arow[:, :], B[4][0:H, 128:128 + S]))
            dve.tensor_tensor_scan(cmrow[:, :], arow[:, :], arow[:, :], 0.0, ALU.max, ALU.max).then_inc(sem("rows_ready"), 1)
            conv(3)

            def normed(first, root, const, done):
                dve.wait_ge(sem("roots_ready"), root)
                r = t1[:, :, :, :].rearrange("p h t i -> p h (t i)")
                link(dve.reciprocal(r, r))
                v = cvg[:, first:first + HC, :]
                dve.scalar_tensor_tensor(out=v, in0=v, scalar=const, in1=r, op0=ALU.mult,
                                         op1=ALU.mult).then_inc(sem(done), 1)

            normed(0, 1, QS, "q_normed")
            dve.wait_ge(sem("decay_spread"), 1)
            for h in range(H):
                for t in range(T):
                    ins = dve.tensor_scalar(decay[:, h, t, :], B[h // 2][:, (h % 2) * S + t * P:(h % 2) * S + (t + 1) * P],
                                            rowsrc[:, t, h:h + 1], 0.0, ALU.subtract, ALU.min)
            ins.then_inc(sem("decay_log"), 1)
            conv(4)
            dve.wait_ge(sem("decay_exp"), 1)
            dve.wait_ge(sem("masks_ready"), 2)
            d8 = decay[:, :, :, :].rearrange("p h t i -> p (h t) i")
            dve.tensor_tensor(d8, d8, bc(triu[:, :].unsqueeze(1), [P, H * T, P]), ALU.mult).then_inc(sem("decay_ready"), 1)
            dve.wait_ge(sem("runmax_turned"), 1)
            dve.scalar_tensor_tensor(out=dmin[:, :, :], in0=B[5][:, 480:480 + T * H].rearrange("p (t h) -> p t h", t=T),
                                     scalar=-1.0, in1=fcum[:, :, :], op0=ALU.mult, op1=ALU.subtract).then_inc(sem("dmin_ready"), 1)
            normed(HC, 2, 1.0, "k_normed")
            conv(5)
            dve.wait_ge(sem("runmax_spread"), 1)
            for h in range(H):
                src = B[4 + h // 2][:, (h % 2) * S:(h % 2 + 1) * S]
                link(dve.tensor_scalar(pt[:, h, 0:2, :].rearrange("p b i -> p (b i)"), src, acol[:, 0, h:h + 1], 0.0,
                                       ALU.subtract, ALU.max))
                ins = dve.tensor_scalar(pt[:, h, 2, :], src[:, P:S], acol[:, 1, h:h + 1], 0.0, ALU.subtract, ALU.max)
            ins.then_inc(sem("pt_log_ready"), 1)
            conv(6)
            dve.wait_ge(sem("k_normed"), 1)
            dve.wait_ge(sem("decay_ready"), 1)
            for b in range(2):
                dve.wait_ge(sem("kk_done"), b + 1)
                v = lt[:, 2 * b:2 * b + 2, :, :].rearrange("p h t i -> p (h t i)")
                link(dve.tensor_tensor(v, B[b], decay[:, 2 * b:2 * b + 2, :, :].rearrange("p h t i -> p (h t i)"), ALU.mult))
                dve.wait_ge(sem("beta_spread"), 1)
                link(dve.tensor_tensor(v, v, B[2 + b], ALU.mult))
            dve.wait_ge(sem("levels_ready"), len(LEVELS))
            l8 = lt[:, :, :, :].rearrange("p h t i -> p (h t) i")
            m8 = ltm[:, :, :, :].rearrange("p h t i -> p (h t) i")

            def mask_level(m):
                dve.tensor_tensor(m8, l8, bc(level[:, m, :].unsqueeze(1), [P, H * T, P]), ALU.mult).then_inc(sem("level_ready"), 1)

            mask_level(0)
            conv(7)
            for b in range(2):
                dve.wait_ge(sem("kq_done"), b + 1)
                ins = dve.tensor_tensor(attn[:, 2 * b:2 * b + 2, :, :].rearrange("p h t i -> p (h t i)"), B[4 + b],
                                        decay[:, 2 * b:2 * b + 2, :, :].rearrange("p h t i -> p (h t i)"), ALU.mult)
            ins.then_inc(sem("attn_ready"), 1)
            dve.wait_ge(sem("pt_exp"), 1)
            v = pt[:, :, 0:3:2, :]
            link(dve.tensor_tensor(v, v, bc(triu[:, :].unsqueeze(1).unsqueeze(1), [P, H, 2, P]), ALU.mult))
            conv(8)

            inv8 = inv[:, :, :, :].rearrange("p h t i -> p (h t) i")
            invT8 = invT[:, :, :, :].rearrange("p h t i -> p (h t) i")
            ib = bc(ident[:, :].unsqueeze(1), [P, H * T, P])
            link(dve.tensor_tensor(invT8, m8, ib, ALU.add))
            for b in range(2):
                dve.wait_ge(sem("t1_done"), b + 1)
                link(dve.tensor_tensor(inv8[:, 4 * b:4 * b + 4, :], B[b].rearrange("p (a i) -> p a i", a=4),
                                       ib[:, 0:4, :], ALU.add))
            mask_level(1)
            for h in range(H):
                dve.wait_ge(sem("ml_kq_done"), h + 1)
                w = pt[:, h, :, :].rearrange("p b i -> p (b i)")
                dve.scalar_tensor_tensor(out=w, in0=B[2 + h][:, 0:3 * P], scalar=QS, in1=w, op0=ALU.mult,
                                         op1=ALU.mult).then_inc(sem("pt_ready"), 1)
            conv(9)

            t18 = t1[:, :, :, :].rearrange("p h t i -> p (h t i)")
            invf = inv[:, :, :, :].rearrange("p h t i -> p (h t i)")
            invTf = invT[:, :, :, :].rearrange("p h t i -> p (h t i)")

            def level_dve(m, between=None):
                for b in range(2):
                    dve.wait_ge(sem("t1_done"), 2 * m + b + 1)
                    ins = dve.tensor_copy(t18[:, b * HALF:(b + 1) * HALF], B[b])
                    if b == 0:
                        link(ins)
                ins.then_inc(sem("t1_ready"), 1)
                if between:
                    between()
                if m < len(LEVELS) - 1:
                    for b in range(2):
                        dve.wait_ge(sem("p_done"), 2 * (m - 1) + b + 1)
                        v = invf[:, b * HALF:(b + 1) * HALF]
                        link(dve.tensor_tensor(v, v, B[2 + b], ALU.add))
                for b in range(2):
                    dve.wait_ge(sem("q_done"), 2 * (m - 1) + b + 1)
                    v = invTf[:, b * HALF:(b + 1) * HALF]
                    ins = dve.tensor_tensor(v, v, B[4 + b], ALU.add)
                    if b == 0:
                        link(ins)
                ins.then_inc(sem("inv_ready"), 1)
                if m < len(LEVELS) - 1:
                    dve.wait_ge(sem("inv_ready"), m)
                    mask_level(m + 1)

            level_dve(1)
            dve.wait_ge(sem("beta_ready"), 1)
            for b in range(2):
                dve.wait_ge(sem("v_turned"), b + 1)
                for hh in range(2):
                    h = 2 * b + hh
                    ins = dve.tensor_tensor(vb[:, h, :, :], B[b][:, hh * S:(hh + 1) * S].rearrange("p (t i) -> p t i", t=T),
                                            bc(rowsrc[:, :, H + h:H + h + 1], [P, T, P]), ALU.mult)
            ins.then_inc(sem("vb_ready"), 1)
            level_dve(2)
            dve.wait_ge(sem("k_turned"), 1)
            dve.wait_ge(sem("ex8_ready"), 1)
            dve.tensor_tensor(kd0[:, :, :], B[0].rearrange("p (h i) -> p h i", h=H),
                              bc(ex8[:, 0:H].unsqueeze(2), [P, H, P]), ALU.mult).then_inc(sem("kd_ready"), 1)
            level_dve(3)

            def mlstm_rows():
                dve.wait_ge(sem("ml_sums_done"), 1)
                dve.wait_ge(sem("dmin_exp"), 1)
                link(dve.tensor_copy(den[:, :, :], B[4][:, 0:T * H].rearrange("p (t h) -> p t h", t=T)))
                link(dve.scalar_tensor_tensor(out=den[:, :, :], in0=den[:, :, :], scalar=-1.0, in1=den[:, :, :],
                                              op0=ALU.mult, op1=ALU.max))
                link(dve.tensor_tensor(den[:, :, :], den[:, :, :], dmin[:, :, :], ALU.max))
                link(dve.reciprocal(den[:, :, :], den[:, :, :]))
                for t in range(T):
                    ins = dve.tensor_tensor(om[:, t, :].rearrange("p (h i) -> p h i", h=H),
                                            B[2 + t].rearrange("p (h i) -> p h i", h=H),
                                            bc(den[:, t, :].unsqueeze(2), [P, H, P]), ALU.mult)
                ins.then_inc(sem("ml_sums_taken"), 1)

            def head_norm(o, scratch, t, norm, gate, col):
                v = o[:, t, :]
                link(dve.tensor_tensor(scratch, v, v, ALU.mult))
                link(dve.tensor_reduce(ss[:, col:col + H], scratch.rearrange("p (h i) -> p h i", h=H), AX.X, ALU.add))

            level_dve(4, mlstm_rows)
            dve.wait_ge(sem("ml_sums_taken"), 1)
            for t in range(T):
                head_norm(om, scr, t, None, None, t * H)
            dve.tensor_scalar(ss[:, :], ss[:, :], 1.0 / DH, NORM_EPS, ALU.mult, ALU.add).then_inc(sem("ml_ms_ready"), 1)
            level_dve(5)
            dve.wait_ge(sem("ml_root"), 1)
            dve.wait_ge(sem("tail_params"), 16 * 5)

            def gated(o, t, norm, gate, done):
                v = o[:, t, :]
                v3 = v.rearrange("p (h i) -> p h i", h=H)
                link(dve.tensor_tensor(v3, v3, bc(rstd[:, t * H:(t + 1) * H].unsqueeze(2), [P, H, P]), ALU.mult))
                link(dve.tensor_tensor(v3, v3, norm, ALU.mult))
                ins = dve.tensor_tensor(v, v, gate[:, t, :], ALU.mult)
                if t == T - 1:
                    ins.then_inc(sem(done), 1)
                else:
                    link(ins)

            link(dve.reciprocal(rstd[:, :], rstd[:, :]))
            dve.wait_ge(sem("proj_taken"), 6)
            for t in range(T):
                gated(om, t, mnorm[:, :].rearrange("p (h i) -> p h i", h=H), mo_s, "om_ready")
            level_dve(6)
            for b in range(2):
                dve.wait_ge(sem("om_turned"), b + 1)
                ins = dve.tensor_copy(cvm[:, 2 * b:2 * b + 2, :].rearrange("p h i -> p (h i)"), B[2 + b])
                if b == 0:
                    link(ins)
            ins.then_inc(sem("omT_ready"), 1)
            dve.wait_ge(sem("u0_done"), 1)
            dve.tensor_copy(ua[:, :, :].rearrange("p h i -> p (h i)"), B[0]).then_inc(sem("u0_ready"), 1)
            dve.wait_ge(sem("state_done"), 1)
            dve.tensor_copy(st[:, :, :].rearrange("p h i -> p (h i)"), B[1]).then_inc(sem("state_ready"), 1)
            dve.wait_ge(sem("o0_done"), 1)
            link(dve.tensor_copy(og[:, 0, :], B[4]))
            link(dve.tensor_tensor(acol[:, 0, :], ex8[:, H:2 * H], rowsrc[:, 1, H:2 * H], ALU.mult))

            def merge_m(i):
                dve.wait_ge(sem("piece_done"), UP_FIRST + i + 1)
                dve.wait_ge(sem("proj_taken"), N_IN - CONV_PIECES)
                for b in range(2):
                    v = gate_m[:, 4 * i + 2 * b:4 * i + 2 * b + 2, :].rearrange("p c s -> p (c s)")
                    ins = dve.tensor_tensor(v, v, B[6 + b], ALU.mult)
                    if b == 0:
                        link(ins)
                ins.then_inc(sem("lift_taken"), 1)

            merge_m(0)
            dve.wait_ge(sem("ks_done"), 1)
            k3 = B[0].rearrange("p (h i) -> p h i", h=H)
            link(dve.tensor_tensor(ub[:, :, :], k3, bc(acol[:, 0, :].unsqueeze(2), [P, H, P]), ALU.mult))
            dve.tensor_tensor(ub[:, :, :], vb[:, :, 1, :], ub[:, :, :], ALU.subtract).then_inc(sem("rhs1_ready"), 1)
            dve.wait_ge(sem("qs_done"), 1)
            og3 = og[:, 1, :].rearrange("p (h i) -> p h i", h=H)
            link(dve.tensor_tensor(og3, B[1].rearrange("p (h i) -> p h i", h=H),
                                   bc(ex8[:, H:2 * H].unsqueeze(2), [P, H, P]), ALU.mult))
            dve.wait_ge(sem("u1_done"), 1)
            dve.tensor_copy(ua[:, :, :].rearrange("p h i -> p (h i)"), B[0]).then_inc(sem("u1_ready"), 1)
            merge_m(1)
            dve.wait_ge(sem("au_done"), 1)
            link(dve.tensor_tensor(og[:, 1, :], og[:, 1, :], B[2], ALU.add))
            for t in range(T):
                head_norm(og, scr, t, None, None, t * H)
            dve.tensor_scalar(ss[:, :], ss[:, :], 1.0 / DH, NORM_EPS, ALU.mult, ALU.add).then_inc(sem("gdn_ms_ready"), 1)
            dve.wait_ge(sem("gdn_root"), 1)
            link(dve.reciprocal(rstd[:, :], rstd[:, :]))
            for t in range(T):
                gated(og, t, bc(gnorm[:, :].unsqueeze(1), [P, H, DH]), z_s, "og_ready")
            for b in range(2):
                dve.wait_ge(sem("og_turned"), b + 1)
                ins = dve.tensor_copy(cvg[:, 2 * HC + 2 * b:2 * HC + 2 * b + 2, :].rearrange("p h i -> p (h i)"), B[4 + b])
                if b == 0:
                    link(ins)
            ins.then_inc(sem("ogT_ready"), 1)
            dve.wait_ge(sem("lift_taken"), 2)
            for i in range(2):
                dve.wait_ge(sem("piece_done"), UP_FIRST + 2 + i + 1)
                for b in range(2):
                    at = slice(4 * i + 2 * b, 4 * i + 2 * b + 2)
                    v = gate_g[:, at, :].rearrange("p c s -> p (c s)")
                    link(dve.tensor_tensor(v, v, B[6 + b], ALU.mult))
                    ins = dve.tensor_tensor(v, v, gate_m[:, at, :].rearrange("p c s -> p (c s)"), ALU.add)
                    if b == 0:
                        link(ins)
                ins.then_inc(sem("lift_taken"), 1)
            dve.wait_ge(sem("piece_done"), MOE_FIRST)
            for t in range(T):
                for n in range(2):
                    v = xs[:, t, n * HALF:(n + 1) * HALF]
                    ins = dve.tensor_tensor(v, v, B[2 * t + n], ALU.add)
                    if n == 0:
                        link(ins)
                ins.then_inc(sem("x2_ready"), 1)
            dve.wait_ge(sem("x2_squared"), T)
            dve.tensor_scalar(ss[:, 0:T], ss[:, 0:T], 1.0 / D, NORM_EPS, ALU.mult, ALU.add).then_inc(sem("ms2_ready"), 1)
            dve.wait_ge(sem("root_x2"), 1)
            link(dve.reciprocal(rstd[:, 0:T], rstd[:, 0:T]))
            for t in range(T):
                signal(dve.tensor_scalar(hn[:, t, :], xs[:, t, :], rstd[:, t:t + 1], None, ALU.mult), "h2_ready")
            fw = lambda k, n, m: bc(prmT[:, 88 + k:88 + k + n].unsqueeze(2), [P, n, m])
            for b in range(2 * T):
                dve.wait_ge(sem("h2_turned"), b + 1)
                t, k = b // 2, 4 * (b % 2)
                signal(dve.tensor_tensor(hT[:, k:k + 4, t * P:(t + 1) * P], B[4 + b].rearrange("p (k i) -> p k i", k=4),
                                         fw(k, 4, P), ALU.mult), "h2T_ready")
            dve.wait_ge(sem("logitsT_done"), 1)
            dve.tensor_copy(eq_rows, B[0][0:E, 0:S]).then_inc(sem("logitsT_ready"), 1)
            dve.wait_ge(sem("logits_done"), 1)
            link(dve.tensor_tensor(lg[:, :, :], B[1][:, 0:T * E].rearrange("p (t e) -> p t e", t=T),
                                   bc(brt[:, :].unsqueeze(1), [P, T, E]), ALU.add))
            for t in range(T):
                link(dve.max(mx8[:, t, :], lg[:, t, :]))
                link(dve.max_index(ix8[:, t, :], mx8[:, t, :], lg[:, t, :]))
            link(dve.tensor_copy(ixf[:, :, :], ix8[:, :, :]))
            dve.tensor_tensor(g4[:, :, :], mx8[:, :, 0:TOP_K], bc(mx8[:, :, 0:1], [P, T, TOP_K]),
                              ALU.subtract).then_inc(sem("top_ready"), 1)
            dve.wait_ge(sem("tables_ready"), TABLES)
            for t in range(T):
                link(dve.tensor_tensor(eq[:, :, :], bc(eiota[:, :].unsqueeze(1), [P, TOP_K, E]),
                                       bc(ixf[:, t, 0:TOP_K].unsqueeze(2), [P, TOP_K, E]), ALU.is_equal))
                link(dve.tensor_reduce(chosen[:, t, :], eq[:, :, :].rearrange("p j e -> p e j"), AX.X, ALU.add))
            dve.memset(posx[:, :, ROUNDS * E:], -1.0).then_inc(sem("chosen_ready"), 1)
            dve.wait_ge(sem("top_exp"), 1)
            link(dve.tensor_reduce(gsum[:, :], g4[:, :, :], AX.X, ALU.add))
            link(dve.reciprocal(gsum[:, :], gsum[:, :]))
            link(dve.tensor_tensor(g4[:, :, :], g4[:, :, :], bc(gsum[:, :].unsqueeze(2), [P, T, TOP_K]), ALU.mult))
            for t in range(T):
                link(dve.tensor_tensor(eq[:, :, :], bc(eiota[:, :].unsqueeze(1), [P, TOP_K, E]),
                                       bc(ixf[:, t, 0:TOP_K].unsqueeze(2), [P, TOP_K, E]), ALU.is_equal))
                link(dve.tensor_tensor(eq[:, :, :], eq[:, :, :], bc(g4[:, t, :].unsqueeze(2), [P, TOP_K, E]), ALU.mult))
                link(dve.tensor_reduce(gates[:, t, :], eq[:, :, :].rearrange("p j e -> p e j"), AX.X, ALU.add))
            link(dve.memset(gatex[:, :, ROUNDS * E:], 0.0))
            for r in range(ROUNDS):
                ins = dve.tensor_copy(gatex[:, :, r * E:(r + 1) * E], gates[:, :, :])
                if r < ROUNDS - 1:
                    link(ins)
            ins.then_inc(sem("gates_ready"), 1)
            dve.wait_ge(sem("chosen_ready"), 1)
            dve.wait_ge(sem("ranks_done"), 1)
            link(dve.scalar_tensor_tensor(out=lg[:, :, :], in0=B[4][:, 0:T * E].rearrange("p (t e) -> p t e", t=T),
                                          scalar=1.0, in1=chosen[:, :, :], op0=ALU.add, op1=ALU.mult))
            for r in range(ROUNDS):
                link(dve.tensor_scalar(posx[:, :, r * E:(r + 1) * E], lg[:, :, :], -1.0 - r * SLOTS, None, ALU.add))
            link(dve.tensor_reduce(cnt[:, 0:1], B[4][:, 2 * E:3 * E], AX.X, ALU.max))
            for r in range(1, ROUNDS):
                link(dve.tensor_scalar(cnt[:, r:r + 1], cnt[:, 0:1], float(r * SLOTS), None, ALU.is_gt))
            link(dve.tensor_reduce(cnt[:, 0:1], cnt[:, 1:ROUNDS], AX.X, ALU.add))
            dve.tensor_scalar(n_pairs[:, :], cnt[:, 0:1], float(PAIRS), float(PAIRS), ALU.mult,
                              ALU.add).then_inc(sem("n_pairs_ready"), 1)

            def make_onehot(n):
                for t in range(T):
                    for e in range(2):
                        dve.tensor_scalar(onehot[:, t, e * SLOTS:(e + 1) * SLOTS], siota[:, :],
                                          posx[:, t, bass.ds(n * 2 + e, 1)], None,
                                          ALU.is_equal).then_inc(sem("onehot_ready"), 1)

            def make_weighted(n):
                for t in range(T):
                    for e in range(2):
                        dve.tensor_scalar(weighted[:, t, e * SLOTS:(e + 1) * SLOTS], siota[:, :],
                                          posx[:, t, bass.ds(n * 2 + e, 1)], gatex[:, t, bass.ds(n * 2 + e, 1)],
                                          ALU.is_equal, ALU.mult).then_inc(sem("weighted_ready"), 1)

            def make_picked(n):
                for e in range(2):
                    dve.tensor_copy(picked[:, e, :], bc(pick[:, bass.ds(n * 2 + e, 1)], [P, SLOTS])).then_inc(sem("picked_ready"), 1)

            def take_xT(n, b, count):
                dve.wait_ge(sem("gathered"), count)
                dve.tensor_tensor(xT[:, 4 * b:4 * b + 4, :], B[6 + b].rearrange("p (k s) -> p k s", k=4),
                                  fw(4 * b, 4, P), ALU.mult).then_inc(sem("xT_ready"), 1)

            def glu(n, e, wait):
                wait()
                if not isinstance(n, int) or e:
                    dve.wait_ge(sem("act_ready"), n * 2 + e)
                both = bank45[:, :, :].rearrange("p b (f two) -> p b f two", two=2)
                g2 = glu_g.rearrange("p (b f) -> p b f", b=2)
                u2 = glu_u.rearrange("p (b f) -> p b f", b=2)
                dve.tensor_scalar(g2, both[:, :, :, 0], SWIGLU_LIMIT, None, ALU.min).then_inc(sem("glu_g_ready"), 1)
                dve.tensor_scalar(u2, both[:, :, :, 1], SWIGLU_LIMIT, -SWIGLU_LIMIT, ALU.min,
                                  ALU.max).then_inc(sem("gu_taken"), 1)
                dve.wait_ge(sem("glu_g_ready"), n * 2 + (e + 1))
                dve.wait_ge(sem("gu_taken"), n * 2 + (e + 1))
                dve.scalar_tensor_tensor(out=glu_u, in0=glu_u, scalar=1.0, in1=glu_g, op0=ALU.add,
                                         op1=ALU.mult).then_inc(sem("glu_u_ready"), 1)
                dve.wait_ge(sem("glu_u_ready"), n * 2 + (e + 1))
                dve.wait_ge(sem("glu_s_ready"), n * 2 + (e + 1))
                dve.tensor_tensor(act[:, e, :], glu_u, glu_s, ALU.mult).then_inc(sem("act_ready"), 1)

            def take_scat(n):
                dve.wait_ge(sem("weighted_turned"), n + 1)
                dve.tensor_copy(scat.rearrange("p t i -> p (t i)"), B[6][:, 0:T * P]).then_inc(sem("scat_ready"), 1)

            def pieces(n, local):
                return lambda: dve.wait_ge(sem("piece_done"), pieces_before(n, local))

            make_onehot(0)
            make_weighted(0)
            make_picked(0)
            take_xT(0, 0, 1)
            take_xT(0, 1, 2)
            dve.wait_ge(sem("gates_turned"), 1)
            dve.tensor_copy(gatesT[:, :], B[5][0:E, 0:S]).then_inc(sem("gatesT_ready"), 1)
            dve.wait_ge(sem("n_pairs_ready"), 1)
            last = dve.value_load(n_pairs[0:1, 0:1], min_val=PAIRS, max_val=PAIRS * ROUNDS)
            make_onehot(1)
            glu(0, 0, lambda: dve.wait_ge(sem("piece_done"), MOE_FIRST + 8))
            glu(0, 1, lambda: dve.wait_ge(sem("piece_done"), MOE_FIRST + 16))
            make_picked(1)
            take_xT(1, 1, 3)
            take_xT(1, 0, 4)
            take_scat(0)
            with dve.Fori(1, last) as n:
                dve.wait_ge(sem("gathered"), n * 2 + 2)
                make_onehot(n + 1)
                make_weighted(n)
                glu(n, 0, pieces(n, 8))
                glu(n, 1, pieces(n, 24))
                make_picked(n + 1)
                take_xT(n + 1, 1, n * 2 + 3)
                take_xT(n + 1, 0, n * 2 + 4)
                take_scat(n)
            dve.wait_ge(sem("sums_done"), 1)
            for t in range(T):
                for h in range(2):
                    v = xs[:, t, h * HALF:(h + 1) * HALF]
                    ins = dve.tensor_tensor(v, v, B[2 * t + h], ALU.add)
                    if h == 0:
                        link(ins)
                ins.then_inc(sem("x3_ready"), 1)
            dve.wait_ge(sem("x3_squared"), T)
            dve.tensor_scalar(ss[:, 0:T], ss[:, 0:T], 1.0 / D, NORM_EPS, ALU.mult, ALU.add).then_inc(sem("ms3_ready"), 1)
            dve.wait_ge(sem("root_x3"), 1)
            link(dve.reciprocal(rstd[:, 0:T], rstd[:, 0:T]))
            for t in range(T):
                dve.scalar_tensor_tensor(out=hn[:, t, :], in0=xs[:, t, :], scalar=rstd[:, t:t + 1], in1=fnorm[:, :],
                                         op0=ALU.mult, op1=ALU.mult).then_inc(sem("result_ready"), 1)

        @block.scalar
        def _(se):
            rows_ = 0
            for src, name in ((gdn_conv, "l w (c p) -> (l w c) p"), (ml_conv, "l w (c p) -> (l w c) p"),
                              (norm_mix, "l (c p) -> (l c) p"), (norm_ffn, "l (c p) -> (l c) p")):
                v = src.rearrange(name, p=P)
                se.dma_start(prm[rows_:rows_ + v.shape[0], :], v).then_inc(sem("prm_loaded"), 16)
                rows_ += v.shape[0]
            se.dma_start(wsc[:, :, 0:2 * H], w_in_v[:, :, c_ga:c_ga + 2 * H]).then_inc(sem("scal_loaded"), 16)
            se.dma_start(wsc[:, :, 2 * H:4 * H], w_in_v[:, :, c_mi:c_mi + 2 * H]).then_inc(sem("scal_loaded"), 16)
            for at, src in ((sbias[:, 0:H], gdn_dt_bias), (sbias[:, 2 * H:3 * H], ml_b_i), (sbias[:, 3 * H:4 * H], ml_b_f),
                            (alog[:, :], gdn_a_log)):
                se.dma_start(at, src.rearrange("l c -> (l c)").partition_broadcast(P)).then_inc(sem("sbias_loaded"), 16)
            se.dma_start(gnorm[:, :], gdn_norm.rearrange("l c -> (l c)").partition_broadcast(P)).then_inc(sem("tail_params"), 16)
            se.dma_start(mnorm[:, :], ml_norm.rearrange("l c -> (l c)").partition_broadcast(P)).then_inc(sem("tail_params"), 16)
            se.dma_start(brt[:, :], b_router.rearrange("l c -> (l c)").partition_broadcast(P)).then_inc(sem("tail_params"), 16)
            se.dma_start(fnorm[:, :], norm_final.partition_broadcast(P)).then_inc(sem("tail_params"), 16)
            se.dma_start(wr[:, :, :], w_router.rearrange("l (k p) e -> p (l k) e", p=P)).then_inc(sem("tail_params"), 16)
            se.wait_ge(sem("bgu_zeroed"), 1)
            se.dma_start(bgu[0:E, :], b_gate_up.rearrange("l e f -> (l e) f")).then_inc(sem("expert_bias"), 16)

            def squares(name):
                for t in range(T):
                    se.activation(hn[:, t, :], xs[:, t, :], ACT.Square, accum_out=ss[:, t:t + 1]).then_inc(sem(name), 1)

            se.wait_ge(sem("x_loaded"), 16)
            squares("x_squared")
            se.wait_ge(sem("ms_ready"), 1)
            se.activation(rstd[:, 0:T], ss[:, 0:T], ACT.Sqrt).then_inc(sem("root_x"), 1)
            se.wait_ge(sem("pre_ready"), 1)
            se.activation(th[:, :, :], pre[:, :, 2 * H:4 * H], ACT.Tanh, scale=1.0 / GATE_SOFTCAP).then_inc(sem("th_ready"), 1)
            se.activation(rowsrc[:, :, H:2 * H], pre[:, :, H:2 * H], ACT.Sigmoid).then_inc(sem("beta_ready"), 1)
            se.wait_ge(sem("a8_ready"), 1)
            se.activation(e8[:, :, :], a8[:, :, :], ACT.Exp, scale=-1.0).then_inc(sem("e8_ready"), 1)
            se.activation(alog[:, :], alog[:, :], ACT.Exp).then_inc(sem("e8_ready"), 1)
            se.wait_ge(sem("e8_ready"), 2)
            se.activation(e8[:, :, :], e8[:, :, :], ACT.Ln, bias=1.0).then_inc(sem("softlog_ready"), 1)

            def tap3(j):
                se.wait_ge(sem("piece_done"), j + 1)
                for c in range(2):
                    i = 2 * j + c
                    if i < 2 * HC:
                        dst, col, stride = cvg[:, i, :], i, 3 * HC
                    elif i < 4 * HC:
                        dst, col, stride = cvm[:, i - 2 * HC, :], 3 * HC * TAPS + i - 2 * HC, 2 * HC
                    else:
                        dst, col, stride = cvg[:, i - 2 * HC, :], i - 2 * HC, 3 * HC
                    at = col + (TAPS - 1) * stride
                    se.activation(dst, B[6 + j % 2][:, c * S:(c + 1) * S], ACT.Identity,
                                  scale=prmT[:, at:at + 1]).then_inc(sem("conv_tap3"), 1)

            def conv_act(j):
                for c in range(2):
                    i = 2 * j + c
                    se.wait_ge(sem("conv_done"), i + 1)
                    dst = cvg[:, i, :] if i < 2 * HC else cvm[:, i - 2 * HC, :] if i < 4 * HC else cvg[:, i - 2 * HC, :]
                    ins = se.activation(dst, dst, ACT.Silu)
                    ins.then_inc(sem("conv_silu"), 1)

            def square(first, n):
                se.wait_ge(sem("conv_silu"), first + HC)
                se.activation(attn[:, :, :, :].rearrange("p h t i -> p h (t i)"), cvg[:, first:first + HC, :],
                              ACT.Square).then_inc(sem("squares_ready"), 1)

            def roots(n):
                se.wait_ge(sem("norm_sums"), n)
                if n == 2:
                    se.wait_ge(sem("q_normed"), 1)
                for b in range(2):
                    ins = se.activation(t1[:, 2 * b:2 * b + 2, :, :].rearrange("p h t i -> p (h t i)"), B[2 + b],
                                        ACT.Sqrt, bias=NORM_EPS)
                ins.then_inc(sem("roots_ready"), 1)

            tap3(0)
            tap3(1)
            conv_act(0)
            conv_act(1)
            square(0, 1)
            se.wait_ge(sem("row_source_ready"), 1)
            se.activation(ex8[:, :], ex8[:, :], ACT.Exp).then_inc(sem("ex8_ready"), 1)
            tap3(2)
            conv_act(2)
            tap3(3)
            roots(1)
            conv_act(3)
            square(HC, 2)
            se.wait_ge(sem("decay_log"), 1)
            se.activation(decay[:, :, :, :].rearrange("p h t i -> p (h t i)"),
                          decay[:, :, :, :].rearrange("p h t i -> p (h t i)"), ACT.Exp).then_inc(sem("decay_exp"), 1)
            tap3(4)
            roots(2)
            conv_act(4)
            tap3(5)
            se.wait_ge(sem("dmin_ready"), 1)
            se.activation(dmin[:, :, :], dmin[:, :, :], ACT.Exp).then_inc(sem("dmin_exp"), 1)
            conv_act(5)
            se.wait_ge(sem("pt_log_ready"), 1)
            se.activation(pt[:, :, :, :].rearrange("p h b i -> p (h b i)"), pt[:, :, :, :].rearrange("p h b i -> p (h b i)"),
                          ACT.Exp, scale=-1.0).then_inc(sem("pt_exp"), 1)
            tap3(6)
            conv_act(6)
            tap3(7)
            conv_act(7)
            se.wait_ge(sem("conv_silu"), 4 * HC)
            se.activation(gsum[:, 0:1], prmT[:, 0:1], ACT.Identity).then_inc(sem("mlstm_qk_ready"), 1)
            tap3(8)
            conv_act(8)
            tap3(9)
            conv_act(9)
            for j in range(CONV_PIECES, N_IN):
                se.wait_ge(sem("piece_done"), j + 1)
                if j < GATE_FIRST:
                    dst, func = ((mv_s, ACT.Identity), (z_s, ACT.Silu), (mo_s, ACT.Sigmoid))[(j - NAT_FIRST) // 2]
                    o = dst[:, :, (j % 2) * PW:(j % 2 + 1) * PW]
                    src = B[6 + j % 2].rearrange("p (t c) -> p t c", t=T)
                else:
                    i = j - GATE_FIRST
                    o = (gate_g if i < 4 else gate_m)[:, 2 * (i % 4):2 * (i % 4) + 2, :].rearrange("p c s -> p (c s)")
                    src, func = B[6 + j % 2], ACT.Sigmoid
                se.activation(o, src, func).then_inc(sem("proj_taken"), 1)
                if j == 18:
                    se.wait_ge(sem("ml_ms_ready"), 1)
                    se.activation(rstd[:, :], ss[:, :], ACT.Sqrt).then_inc(sem("ml_root"), 1)
            se.wait_ge(sem("gdn_ms_ready"), 1)
            se.activation(rstd[:, :], ss[:, :], ACT.Sqrt).then_inc(sem("gdn_root"), 1)
            se.wait_ge(sem("x2_ready"), T)
            se.dma_start(bdn, b_down.rearrange("l e d -> (l e) d")).then_inc(sem("bdn_loaded"), 16)
            squares("x2_squared")
            se.wait_ge(sem("ms2_ready"), 1)
            se.activation(rstd[:, 0:T], ss[:, 0:T], ACT.Sqrt).then_inc(sem("root_x2"), 1)
            se.wait_ge(sem("top_ready"), 1)
            se.activation(g4[:, :, :], g4[:, :, :], ACT.Exp).then_inc(sem("top_exp"), 1)

            def sigmoid(n, e):
                se.wait_ge(sem("glu_g_ready"), n * 2 + (e + 1))
                if isinstance(n, int):
                    if e:
                        se.wait_ge(sem("act_ready"), 1)
                else:
                    se.wait_ge(sem("act_ready"), n * 2 + e)
                se.activation(glu_s, glu_g, ACT.Sigmoid, scale=SWIGLU_ALPHA).then_inc(sem("glu_s_ready"), 1)

            def take_turned(n, e):
                se.wait_ge(sem("act_turned"), n * 2 + (e + 1))
                se.activation(actT[:, e, :], B[6 + e], ACT.Identity).then_inc(sem("turned_copied"), 1)

            def take_y(done):
                se.wait_ge(sem("piece_done"), done)
                for half in range(2):
                    se.activation(ysb[:, half * HALF:(half + 1) * HALF], B[6 + half], ACT.Identity).then_inc(sem("y_copied"), 1)

            se.wait_ge(sem("n_pairs_ready"), 1)
            last = se.value_load(n_pairs[0:1, 0:1], min_val=PAIRS, max_val=PAIRS * ROUNDS)
            sigmoid(0, 0)
            take_turned(0, 0)
            sigmoid(0, 1)
            take_turned(0, 1)
            with se.Fori(1, last) as n:
                sigmoid(n, 0)
                take_y(pieces_before(n, 16))
                sigmoid(n, 1)
                take_turned(n, 0)
                take_turned(n, 1)
            take_y(pieces_before(last, 8))
            se.wait_ge(sem("x3_ready"), T)
            squares("x3_squared")
            se.wait_ge(sem("ms3_ready"), 1)
            se.activation(rstd[:, 0:T], ss[:, 0:T], ACT.Sqrt).then_inc(sem("root_x3"), 1)


_INS = ["x", "norm_mix", "w_in", "gdn_conv", "gdn_a_log", "gdn_dt_bias", "gdn_norm", "ml_conv", "ml_b_i", "ml_b_f",
        "ml_norm", "w_up_gdn", "w_up_ml", "w_out", "norm_ffn", "w_router", "b_router", "w_gate_up", "b_gate_up",
        "w_down", "b_down", "norm_final"]


def kernel(**inputs):
    import numpy as np
    import concourse.bacc as bacc
    from concourse.bass_utils import run_bass_kernel_spmd

    nc = bacc.Bacc("TRN2", target_bir_lowering=False, num_devices=1)
    arrays, args = {}, []
    for name in _INS:
        a = np.ascontiguousarray(inputs[name])
        arrays[f"in_{name}"] = a
        args.append(nc.dram_tensor(f"in_{name}", a.shape, mybir.dt.from_np(a.dtype), kind="ExternalInput").ap())
    out = nc.dram_tensor("out_0", inputs["x"].shape, F32, kind="ExternalOutput").ap()
    decoder_layer(nc, *args, out)
    r = run_bass_kernel_spmd(nc, [arrays], core_ids=[0])
    return r.results[0]["out_0"]
```

```python
from contextlib import ExitStack

import concourse.bass as bass
from concourse import mybir

F32 = mybir.dt.float32
I32 = mybir.dt.int32
U32 = mybir.dt.uint32
ALU = mybir.AluOpType
ACT = mybir.ActivationFunctionType
AX = mybir.AxisListType

P = 128
GATE_SOFTCAP = 15.0
SWIGLU_LIMIT = 7.0
SWIGLU_ALPHA = 1.702
TOP_K = 4
NORM_EPS = 1e-6
HALF = 512
SLOTS = 64
RING = 8
EXPERT_RING = 12
PIECE = 2048
TAPS = 4


def decoder_layer(nc, x, norm_mix, w_in, gdn_conv, gdn_a_log, gdn_dt_bias, gdn_norm, ml_conv,
                  ml_b_i, ml_b_f, ml_norm, w_up_gdn, w_up_ml, w_out, norm_ffn, w_router,
                  b_router, w_gate_up, b_gate_up, w_down, b_down, norm_final, out):
    _, S, D = x.shape
    E = w_router.shape[2]
    FE = w_down.shape[2]
    H = gdn_a_log.shape[1]
    DH = gdn_norm.shape[1]
    T = S // P
    KC = D // P
    HC = H * DH // P
    assert DH == P and T == 2 and D == 1024 and FE == D and H == 4 and E == 32
    PAIRS = E // 2
    MORE = S // SLOTS - 1
    EXTRA = 16
    assert S * TOP_K // (SLOTS + 1) < EXTRA + 1 and EXTRA % 2 == 0
    MOST_PAIRS = (E + EXTRA) // 2
    QS = float(DH) ** -0.5

    width = H * DH
    c_gq, c_gk, c_gv, c_gz = 0, width, 2 * width, 3 * width
    c_ga = 4 * width
    c_gb = c_ga + H
    c_mq = c_gb + H
    c_mk, c_mv, c_mo = c_mq + width, c_mq + 2 * width, c_mq + 3 * width
    c_mi = c_mq + 4 * width
    c_gg = c_mi + 2 * H
    c_gm = c_gg + D
    PW = PIECE // KC
    in_cols = [c + PW * i for c, n in ((c_gq, 2), (c_gk, 2), (c_mq, 2), (c_mk, 2), (c_gv, 2), (c_mv, 2),
                                       (c_gz, 2), (c_mo, 2), (c_gg, 4), (c_gm, 4)) for i in range(n)]
    N_IN = len(in_cols)
    CONV_PIECES, NAT_FIRST, GATE_FIRST = 10, 10, 16
    UP_FIRST = N_IN
    OUT_FIRST = UP_FIRST + 4
    MOE_FIRST = OUT_FIRST + 4
    PER_PAIR = 24
    assert MOE_FIRST % RING == 0 and PER_PAIR % EXPERT_RING == 0

    with ExitStack() as ctx:
        def sb(name, shape, dt=F32):
            return ctx.enter_context(nc.sbuf_tensor(name, shape, dt))

        sems = {}

        def sem(name):
            if name not in sems:
                sems[name] = ctx.enter_context(nc.semaphore(name))
            return sems[name]

        ring = sb("ring", [P, EXPERT_RING, PIECE])
        late = [ring[:, RING + i // 2, (i % 2) * T * width:(i % 2 + 1) * T * width] for i in range(8)]
        rows4 = lambda v: v.rearrange("p (t c) -> p t c", t=T)
        head4 = lambda v: v.rearrange("p (h t i) -> p h t i", h=H, t=T)
        xs = sb("xs", [P, T, D])
        hn = sb("hn", [P, T, D])
        hT = sb("hT", [P, KC, S])
        cvg = sb("cvg", [P, 3 * HC, S])
        cvm = sb("cvm", [P, 2 * HC, S])
        gate_g = sb("gate_g", [P, KC, S])
        gate_m = sb("gate_m", [P, KC, S])
        z_s, mo_s, mv_s = rows4(late[0]), rows4(late[1]), rows4(late[2])
        intra = sb("intra", [P, 5 * H * P])
        decay = intra[:, 0:T * H * P].rearrange("p (h t i) -> p h t i", h=H, t=T)
        pt = intra[:, T * H * P:].rearrange("p (h b i) -> p h b i", h=H, b=3)
        lt = head4(late[3])
        ltm = sb("ltm", [P, H, T, P])
        inv, invT = head4(late[4]), head4(late[5])
        t1 = head4(late[6])
        attn = head4(late[7])
        vb = sb("vb", [P, H, T, P])
        kd0 = sb("kd0", [P, H, P])
        ua = lt[:, 0:2, :, :].rearrange("p h t i -> p (h t) i")
        ub = lt[:, 2:4, :, :].rearrange("p h t i -> p (h t) i")
        st = ltm[:, 0:2, :, :].rearrange("p h t i -> p (h t) i")
        om = hn[:, 0, :].rearrange("p (t c) -> p t c", t=T)
        og = hn[:, 1, :].rearrange("p (t c) -> p t c", t=T)
        scal_rows = ltm[0:4 * H, 0, :, :].rearrange("p t i -> p (t i)")
        scr = cvm[:, 2 * HC - 2:2 * HC, :].rearrange("p a s -> p (a s)")
        ident = sb("ident", [P, P])
        triu = sb("triu", [P, P])
        striu = sb("striu", [P, P])
        ones = sb("ones", [P, P])
        LEVELS = [1 << s for s in range(7)]
        level = sb("level", [P, len(LEVELS), P])
        prm = sb("prm", [96, P])
        prmT = sb("prmT", [P, 96])
        wsc = sb("wsc", [P, KC, 4 * H])
        sbias = sb("sbias", [P, 4 * H])
        alog = sb("alog", [P, H])
        gnorm = sb("gnorm", [P, DH])
        mnorm = sb("mnorm", [P, width])
        fnorm = sb("fnorm", [P, D])
        brt = sb("brt", [P, E])
        wr = sb("wr", [P, KC, E])
        bgu = sb("bgu", [P, 2 * FE])
        pre = sb("pre", [P, T, 4 * H])
        th = sb("th", [P, T, 2 * H])
        q8 = sb("q8", [P, T, 2 * H])
        a8 = sb("a8", [P, T, 2 * H])
        e8 = sb("e8", [P, T, 2 * H])
        g8 = sb("g8", [P, T, 2 * H])
        rowsrc = sb("rowsrc", [P, T, 2 * H])
        fcum = sb("fcum", [P, T, H])
        acol = sb("acol", [P, T, H])
        ex8 = sb("ex8", [P, 2 * H])
        rows = sb("rows", [2 * H, S])
        arow = sb("arow", [H, S])
        cmrow = sb("cmrow", [H, S])
        dmin = sb("dmin", [P, T, H])
        den = sb("den", [P, T, H])
        ss = sb("ss", [P, 2 * H])
        rstd = sb("rstd", [P, 2 * H])
        lg = sb("lg", [P, T, E])
        mx8 = sb("mx8", [P, T, 8])
        ix8 = sb("ix8", [P, T, 8], U32)
        ixf = sb("ixf", [P, T, 8])
        g4 = sb("g4", [P, T, TOP_K])
        gsum = sb("gsum", [P, T])
        eiota = sb("eiota", [P, E])
        siota = sb("siota", [P, SLOTS])
        chosen = sb("chosen", [P, T, E])
        gates = sb("gates", [P, T, E])
        dead_k = kd0[:, :, :].rearrange("p h i -> p (h i)")
        gatesT = dead_k[0:E, 0:S]
        cnt = sb("cnt", [P, 4])
        n_pairs = sb("n_pairs", [P, 2], I32)
        XCOLS = E + EXTRA + 2
        posx = sb("posx", [P, T, XCOLS])
        gatex = sb("gatex", [P, T, XCOLS])
        pick = sb("pick", [P, XCOLS])
        ids = sb("ids", [1, XCOLS], I32)
        ecol = sb("ecol", [P, 1])
        rankT = vb[0:E, 0, :, :].rearrange("p t i -> p (t i)")
        eq = dead_k[:, S:S + T * TOP_K * E].rearrange("p (t j e) -> p t j e", t=T, j=TOP_K)
        again = sb("again", [E, MORE])
        cntc = sb("cntc", [E, 1])
        order = sb("order", [E, MORE])
        totals = sb("totals", [P, MORE])
        place = sb("place", [E, MORE, EXTRA])
        placed = sb("placed", [E, EXTRA])
        shift = sb("shift", [E, EXTRA])
        half_n = sb("half_n", [P, EXTRA // 2])

        bank = [ctx.enter_context(nc.psum_tensor(f"bank{i}", [P, HALF], F32)) for i in range(4)]
        bank45 = ctx.enter_context(nc.psum_tensor("bank45", [P, 2, HALF], F32))
        bank67 = ctx.enter_context(nc.psum_tensor("bank67", [P, 2, HALF], F32))
        B = [b[:, :] for b in bank] + [bank45[:, 0, :], bank45[:, 1, :], bank67[:, 0, :], bank67[:, 1, :]]

        onehot = ltm[:, 0, :, :]
        weighted = ltm[:, 1, :, :]
        scat = ltm[:, 2, :, :]
        picked = ltm[:, 3, :, :].rearrange("p t (a s) -> p t a s", a=2)[:, 0, :, :]
        xT = cvg[:, 0:4, :].rearrange("p a (b s) -> p (a b) s", b=2)
        act = cvg[:, 4:8, :].rearrange("p (e a) s -> p e (a s)", e=2)
        actT = cvg[:, 8:12, :].rearrange("p (e a) s -> p e (a s)", e=2)
        glu_g = cvm[:, 0:2, :].rearrange("p a s -> p (a s)")
        glu_u = cvm[:, 2:4, :].rearrange("p a s -> p (a s)")
        glu_s = cvm[:, 4:6, :].rearrange("p a s -> p (a s)")
        scat_left = decay[:, 0, :, :]
        actT_left = act[:, 1, :]
        ysb = vb[:, :, :, :].rearrange("p h t i -> p (h t i)")

        bdn = intra[0:E, 0:D]
        logitsT = dead_k[0:E, 0:S]
        flat = lambda v: v[:, :, :].rearrange("p a s -> p (a s)")
        once = {0: intra[:, 0:PIECE], 9: flat(gate_m), 14: flat(gate_g), 15: flat(hT)}

        def landed(eng, j):
            eng.wait_ge(sem(f"ring_full{j % RING}"), 16 * (j // RING + 1))

        BEFORE = MOE_FIRST // RING

        ring_order = [0, 1] + list(range(RING, EXPERT_RING)) + list(range(2, RING))

        def turn_of(n, local):
            return local - len([i for i in once if i < local]) if isinstance(n, int) and n == 0 else local

        def slot(n, local):
            if isinstance(n, int) and n == 0 and local in once:
                return once[local]
            return ring[:, ring_order[turn_of(n, local) % EXPERT_RING], :]

        def landed_in_pair(eng, n, local):
            if isinstance(n, int) and n == 0 and local in once:
                eng.wait_ge(sem(f"once_full{local}"), 16)
                return
            s = ring_order[turn_of(n, local) % EXPERT_RING]
            before = BEFORE if s < RING else 0
            if isinstance(n, int) and n == 0:
                eng.wait_ge(sem(f"ring_full{s}"), 16 * (before + 1))
            else:
                eng.wait_ge(sem(f"ring_full{s}"), n * 32 + 16 * (before + local // EXPERT_RING))

        def pieces_before(n, local):
            return n * PER_PAIR + (MOE_FIRST + 2 * 8 - PER_PAIR + local)

        def pair_counts(eng):
            return (eng.value_load(n_pairs[0:1, 0:1], min_val=PAIRS, max_val=MOST_PAIRS),
                    eng.value_load(n_pairs[0:1, 1:2], min_val=0, max_val=1))

        w_in_v = w_in.rearrange("l (k p) c -> p (l k) c", p=P)
        up_v = [w.rearrange("l (k p) c -> p (l k) c", p=P) for w in (w_up_ml, w_up_gdn)]
        out_v = w_out.rearrange("l (k p) c -> p (l k) c", p=P)
        gu_v = w_gate_up.rearrange("l e (k p) c -> (l e) p k c", p=P)
        dn_v = w_down.rearrange("l e (k p) c -> (l e) p k c", p=P)

        def by_block(place, k):
            return place.rearrange("p (k c) -> p k c", k=k)

        def slot3(s, k):
            return by_block(ring[:, s, :], k)

        block = ctx.enter_context(nc.Block())

        @block.sync
        def _(sp):
            for t in range(T):
                sp.dma_start(xs[:, t, :], x.rearrange("b (t p) d -> p (b t) d", p=P)[:, t, :]).then_inc(sem(f"x{t}_loaded"), 16)
            at = 0
            for src, name in ((gdn_conv, "l w (c p) -> (l w c) p"), (ml_conv, "l w (c p) -> (l w c) p"),
                              (norm_mix, "l (c p) -> (l c) p"), (norm_ffn, "l (c p) -> (l c) p")):
                v = src.rearrange(name, p=P)
                sp.dma_start(prm[at:at + v.shape[0], :], v).then_inc(sem("prm_loaded"), 16)
                at += v.shape[0]
            for dst, src in ((sbias[:, 0:H], gdn_dt_bias), (sbias[:, 2 * H:3 * H], ml_b_i), (sbias[:, 3 * H:4 * H], ml_b_f),
                            (alog[:, :], gdn_a_log)):
                sp.dma_start(dst, src.rearrange("l c -> (l c)").partition_broadcast(P)).then_inc(sem("sbias_loaded"), 16)

            def put(s, src, k):
                sp.dma_start(slot3(s, k), src).then_inc(sem(f"ring_full{s}"), 16)

            for j in range(MOE_FIRST):
                if j >= RING:
                    sp.wait_ge(sem("piece_done"), j - RING + 1)
                if j < N_IN:
                    put(j % RING, w_in_v[:, :, in_cols[j]:in_cols[j] + PW], KC)
                elif j < OUT_FIRST:
                    i = j - UP_FIRST
                    put(j % RING, up_v[i // 2][:, :, (i % 2) * HALF:(i % 2 + 1) * HALF], HC)
                else:
                    i = j - OUT_FIRST
                    put(j % RING, out_v[:, 2 * i:2 * i + 2, :], 2)

            def room(n, local):
                if isinstance(n, int) and n == 0:
                    s = None if local in once else ring_order[turn_of(0, local)]
                    if local == 0:
                        sp.wait_ge(sem("ml_sums_taken"), 1)
                    elif local == 9:
                        sp.wait_ge(sem("lift_taken"), 4)
                    elif local == 14:
                        sp.wait_ge(sem("piece_done"), MOE_FIRST)
                    elif local == 15:
                        sp.wait_ge(sem("logitsT_done"), 1)
                    elif s < RING:
                        sp.wait_ge(sem("piece_done"), MOE_FIRST - RING + s + 1)
                    else:
                        sp.wait_ge(sem("og_ready"), T)
                elif isinstance(n, int) and n == 1 and local < EXPERT_RING:
                    last_in_place = [i for i in range(16) if i not in once][local]
                    sp.wait_ge(sem("piece_done"), MOE_FIRST + last_in_place + 1)
                else:
                    sp.wait_ge(sem("piece_done"), pieces_before(n, local) - EXPERT_RING + 1)

            def fetch(n, local, src, k):
                room(n, local)
                own = isinstance(n, int) and n == 0 and local in once
                full = f"once_full{local}" if own else f"ring_full{ring_order[turn_of(n, local) % EXPERT_RING]}"
                sp.dma_start(by_block(slot(n, local), k), src).then_inc(sem(full), 16)

            def gate_up(n, e, local):
                for k in range(KC):
                    fetch(n, local + k, gu_v[bass.ds(e, 1), :, k, :].rearrange("e p c -> p e c"), 1)

            def down(n, pair_of, local):
                for i in range(8):
                    fetch(n, local + i,
                          dn_v[bass.ds(pair_of[i % 2], 1), :, 2 * (i // 2):2 * (i // 2) + 2, :].rearrange("e p k c -> p (e k) c"), 2)

            def item(i):
                return sp.value_load(ids[0:1, bass.ds(i, 1)], min_val=0, max_val=E - 1)

            gate_up(0, 0, 0)
            gate_up(0, 1, 8)
            gate_up(1, 2, 0)
            down(1, (0, 1), 8)
            gate_up(1, 3, 16)
            with sp.Fori(2, PAIRS) as n:
                gate_up(n, n * 2, 0)
                down(n, (n * 2 - 2, n * 2 - 1), 8)
                gate_up(n, n * 2 + 1, 16)
            sp.wait_ge(sem("items_ready"), 1)
            pairs, odd = pair_counts(sp)
            with sp.If(pairs > PAIRS):
                with sp.Fori(PAIRS, pairs) as n:
                    gate_up(n, item(n * 2), 0)
                    down(n, (item(n * 2 - 2), item(n * 2 - 1)), 8)
                    gate_up(n, item(n * 2 + 1), 16)
            with sp.If(odd < 1):
                down(pairs, (item(pairs * 2 - 2), item(pairs * 2 - 1)), 0)
            with sp.If(odd > 0):
                single = item(pairs * 2)
                gate_up(pairs, single, 0)
                down(pairs, (item(pairs * 2 - 2), item(pairs * 2 - 1)), 8)
                for i in range(4):
                    fetch(pairs, 16 + i,
                          dn_v[bass.ds(single, 1), :, 2 * i:2 * i + 2, :].rearrange("e p k c -> p (e k) c"), 2)
            for t in range(T):
                sp.wait_ge(sem("result_ready"), t + 1)
                sp.dma_start(out.rearrange("b (t p) d -> p (b t) d", p=P)[:, t, :], hn[:, t, :]).then_inc(sem("stored"), 16)
            sp.wait_ge(sem("stored"), 16 * T)

        @block.gpsimd
        def _(pool):
            n = [0]

            def link(ins):
                n[0] += 1
                ins.then_inc(sem("pool_step"), 1)
                pool.wait_ge(sem("pool_step"), n[0])

            link(pool.memset(ident[:, :], 0.0))
            pool.affine_select(out=ident[:, :], in_=ident[:, :], compare_op=ALU.not_equal, fill=1.0, base=0,
                               pattern=[[-1, P]], channel_multiplier=1).then_inc(sem("ident_ready"), 1)
            link(pool.memset(ones[:, :], 1.0))
            pool.affine_select(out=triu[:, :], in_=ones[:, :], compare_op=ALU.is_ge, fill=0.0, base=0,
                               pattern=[[1, P]], channel_multiplier=-1).then_inc(sem("masks_ready"), 1)
            pool.affine_select(out=striu[:, :], in_=ones[:, :], compare_op=ALU.is_ge, fill=0.0, base=-1,
                               pattern=[[1, P]], channel_multiplier=-1).then_inc(sem("masks_ready"), 1)
            link(pool.memset(level[:, :, :], 0.0))
            for m, s in enumerate(LEVELS):
                v = level[:, m, :].rearrange("p (b h r) -> p b h r", h=2, r=s)[:, :, 1, :]
                link(pool.memset(v, -1.0))
                link(pool.affine_select(out=v, in_=v, compare_op=ALU.is_ge, fill=0.0, base=0,
                                        pattern=[[-2 * s, P // (2 * s)], [0, s]], channel_multiplier=1))
                pool.affine_select(out=v, in_=v, compare_op=ALU.is_ge, fill=0.0, base=s - 1,
                                   pattern=[[2 * s, P // (2 * s)], [0, s]],
                                   channel_multiplier=-1).then_inc(sem("levels_ready"), 1)
            pool.iota(eiota[:, :], [[1, E]], base=0, channel_multiplier=0,
                      allow_small_or_imprecise_dtypes=True).then_inc(sem("tables_ready"), 1)
            pool.iota(siota[:, :], [[1, SLOTS]], base=0, channel_multiplier=0,
                      allow_small_or_imprecise_dtypes=True).then_inc(sem("tables_ready"), 1)
            pool.wait_ge(sem("ident_ready"), 1)
            pool.tensor_copy(pick[:, 0:E], ident[:, 0:E]).then_inc(sem("tables_ready"), 1)
            pool.memset(pick[:, E:], 0.0).then_inc(sem("tables_ready"), 1)
            pool.iota(ecol[:, :], [[1, 1]], base=0, channel_multiplier=1,
                      allow_small_or_imprecise_dtypes=True).then_inc(sem("tables_ready"), 1)
            pool.memset(bgu[:, :], 0.0).then_inc(sem("bgu_zeroed"), 1)

        TABLES = 5

        @block.tensor
        def _(pe):
            def proj(j):
                dst = B[6 + j % 2]
                landed(pe, j)
                if 2 <= j <= CONV_PIECES + 1:
                    pe.wait_ge(sem("conv_done"), 2 * (j - 1))
                if j >= CONV_PIECES + 2:
                    pe.wait_ge(sem("proj_taken"), j - 1 - CONV_PIECES)
                w = slot3(j % RING, KC)
                for c in range(2):
                    for k in range(KC):
                        if NAT_FIRST <= j < GATE_FIRST:
                            lhs, rhs = hT[:, k, c * P:(c + 1) * P], w[:, k, :]
                        else:
                            lhs, rhs = w[:, k, c * P:(c + 1) * P], hT[:, k, :]
                        mm = pe.matmul(dst[:, c * S:(c + 1) * S], lhs, rhs, start=(k == 0), stop=(k == KC - 1))
                mm.then_inc(sem("piece_done"), 1)

            def transposes(src, banks, signal):
                for i, s in enumerate(src):
                    mm = pe.transpose(B[banks[i // 4]][:, (i % 4) * P:(i % 4 + 1) * P], s, ident[:, :])
                    if i % 4 == 3 or i == len(src) - 1:
                        mm.then_inc(sem(signal), 1)

            def per_head(banks, signal, product):
                for h in range(H):
                    for t in range(T):
                        i = h * T + t
                        lhs, rhs = product(h, t)
                        mm = pe.matmul(B[banks[i // 4]][:, (i % 4) * P:(i % 4 + 1) * P], lhs, rhs, start=True, stop=True)
                        if i % 4 == 3:
                            mm.then_inc(sem(signal), 1)

            def chunk_products(bnk, signal, product):
                for h in range(H):
                    lhs, rhs = product(h)
                    mm = pe.matmul(B[bnk][:, h * P:(h + 1) * P], lhs, rhs, start=True, stop=True)
                mm.then_inc(sem(signal), 1)

            pe.wait_ge(sem("ident_ready"), 1)
            def keep_busy(n):
                for i in range(n):
                    pe.matmul(B[7][:, 0:P], ident[:, :], ident[:, :], start=True, stop=True)

            keep_busy(12)
            pe.wait_ge(sem("prm_loaded"), 64)
            pe.transpose(B[4][:, 0:96], prm[:, :], ident[0:96, 0:96]).then_inc(sem("prm_turned"), 1)
            keep_busy(8)
            for t in range(T):
                pe.wait_ge(sem("hn_ready"), t + 1)
                transposes([hn[:, t, k * P:(k + 1) * P] for k in range(KC)], [2 * t, 2 * t + 1], "h_turned")
            pe.wait_ge(sem("scal_loaded"), 32)
            pe.wait_ge(sem("hT_ready"), 2 * T)
            for k in range(KC):
                mm = pe.matmul(B[5][0:4 * H, 128:128 + S], wsc[:, k, :], hT[:, k, :], start=(k == 0), stop=(k == KC - 1))
            mm.then_inc(sem("scal_rows_done"), 1)
            pe.wait_ge(sem("scal_rows_ready"), 1)
            for t in range(T):
                mm = pe.transpose(B[5][:, t * 4 * H:(t + 1) * 4 * H], scal_rows[:, t * P:(t + 1) * P], ident[0:4 * H, 0:4 * H])
            mm.then_inc(sem("scal_done"), 1)
            proj(0)
            proj(1)
            pe.wait_ge(sem("masks_ready"), 2)
            pe.wait_ge(sem("log_decay_ready"), 2)
            pe.matmul(B[5][:, 64:64 + 2 * H], triu[:, :], g8[:, 0, :], start=True, stop=True)
            pe.matmul(B[5][:, 64 + 2 * H:64 + 4 * H], triu[:, :], g8[:, 1, :], start=True, stop=False,
                      skip_group_check=True)
            pe.matmul(B[5][:, 64 + 3 * H:64 + 4 * H], ones[:, :], g8[:, 0, H:2 * H], start=False, stop=True,
                      skip_group_check=True)
            pe.matmul(B[5][:, 96:96 + H], ones[:, :], g8[:, 0, 0:H], start=True, stop=True,
                      skip_group_check=True).then_inc(sem("cum_done"), 1)
            proj(2)
            pe.wait_ge(sem("row_source_ready"), 1)
            for t in range(T):
                pe.transpose(B[5][0:2 * H, 128 + t * P:128 + (t + 1) * P], rowsrc[:, t, :], ident[:, :])
            for t in range(T):
                mm = pe.transpose(B[4][0:H, 128 + t * P:128 + (t + 1) * P], acol[:, t, :], ident[:, :])
            mm.then_inc(sem("rows_turned"), 1)
            proj(3)
            pe.wait_ge(sem("squares_ready"), 1)
            for i in range(HC):
                mm = pe.matmul(B[2 + i // 2][:, (i % 2) * S:(i % 2 + 1) * S], ones[:, :], attn[:, i, :, :],
                               start=True, stop=True)
            mm.then_inc(sem("norm_sums"), 1)
            pe.wait_ge(sem("rows_ready"), 1)
            for t in range(T):
                mm = pe.transpose(B[5][:, 480 + t * H:480 + (t + 1) * H], cmrow[:, t * P:(t + 1) * P], ident[0:H, 0:H])
            mm.then_inc(sem("runmax_turned"), 1)

            def spread(src, first, banks, signal):
                n = src.shape[0]
                for h in range(H):
                    mm = pe.matmul(B[banks[h // 2]][:, (h % 2) * S:(h % 2 + 1) * S],
                                   ident[0:n, first + h:first + h + 1].to_broadcast([n, P]), src[:, :],
                                   start=True, stop=True)
                mm.then_inc(sem(signal), 1)

            pe.wait_ge(sem("hT_ready"), 2 * T)
            spread(rows, 0, (0, 1), "decay_spread")
            proj(4)
            pe.wait_ge(sem("squares_ready"), 2)
            pe.wait_ge(sem("roots_ready"), 1)
            for i in range(HC):
                mm = pe.matmul(B[2 + i // 2][:, (i % 2) * S:(i % 2 + 1) * S], ones[:, :], attn[:, i, :, :],
                               start=True, stop=True)
            mm.then_inc(sem("norm_sums"), 1)
            proj(5)
            pe.wait_ge(sem("roots_ready"), 2)
            spread(rows, H, (2, 3), "beta_spread")
            pe.wait_ge(sem("dmin_ready"), 1)
            spread(cmrow, 0, (4, 5), "runmax_spread")
            proj(6)
            pe.wait_ge(sem("k_normed"), 1)
            pe.wait_ge(sem("decay_ready"), 1)
            kT = lambda h, t: cvg[:, HC + h, t * P:(t + 1) * P]
            qT = lambda h, t: cvg[:, h, t * P:(t + 1) * P]
            per_head((0, 1), "kk_done", lambda h, t: (kT(h, t), kT(h, t)))
            proj(7)
            pe.wait_ge(sem("q_normed"), 1)
            pe.wait_ge(sem("pt_log_ready"), 1)
            per_head((4, 5), "kq_done", lambda h, t: (kT(h, t), qT(h, t)))
            proj(8)
            def level_t1(m):
                pe.wait_ge(sem("level_ready"), m + 1)
                per_head((0, 1), "t1_done",
                         lambda h, t: (ltm[:, h, t, :], ident[:, :] if m == 0 else inv[:, h, t, :]))

            def level_pq(m):
                pe.wait_ge(sem("t1_ready"), m)
                if m < len(LEVELS) - 1:
                    per_head((2, 3), "p_done", lambda h, t: (invT[:, h, t, :], t1[:, h, t, :]))
                per_head((4, 5), "q_done", lambda h, t: (t1[:, h, t, :], invT[:, h, t, :]))

            level_t1(0)
            proj(9)
            pe.wait_ge(sem("mlstm_qk_ready"), 1)
            pe.wait_ge(sem("attn_ready"), 1)
            pe.wait_ge(sem("level_ready"), 1)
            for h in range(H):
                pe.matmul(B[2 + h][:, 0:S], cvm[:, HC + h, 0:P], cvm[:, h, :], start=True, stop=True)
                pe.matmul(B[2 + h][:, S:S + P], cvm[:, HC + h, P:S], cvm[:, h, P:S], start=True,
                          stop=True).then_inc(sem("ml_kq_done"), 1)
            proj(10)
            level_t1(1)
            proj(11)
            pe.wait_ge(sem("pt_ready"), H)
            level_pq(1)
            pe.wait_ge(sem("conv_silu"), 3 * HC + 2 * HC)
            transposes([cvg[:, 2 * HC + h, t * P:(t + 1) * P] for h in range(H) for t in range(T)], (0, 1), "v_turned")
            proj(12)
            pe.wait_ge(sem("vb_ready"), 1)
            level_t1(2)
            proj(13)
            level_pq(2)
            transposes([kT(h, 0) for h in range(H)], (0,), "k_turned")
            proj(14)
            pe.wait_ge(sem("kd_ready"), 1)
            level_t1(3)
            proj(15)
            level_pq(3)
            proj(16)
            level_t1(4)
            pe.wait_ge(sem("proj_taken"), 2)
            pe.wait_ge(sem("inv_ready"), 3)
            for t in range(T):
                for h in range(H):
                    for j in range(t + 1):
                        w = pt[:, h, t + j, :]
                        pe.matmul(B[2 + t][:, h * P:(h + 1) * P], w, mv_s[:, j, h * DH:(h + 1) * DH],
                                  start=(j == 0), stop=(j == t))
            for t in range(T):
                for h in range(H):
                    for j in range(t + 1):
                        mm = pe.matmul(B[4][:, t * H + h:t * H + h + 1], pt[:, h, t + j, :], ones[:, 0:1],
                                       start=(j == 0), stop=(j == t))
            mm.then_inc(sem("ml_sums_done"), 1)
            proj(17)
            pe.wait_ge(sem("ml_sums_taken"), 1)
            level_pq(4)
            proj(18)
            level_t1(5)
            proj(19)
            level_pq(5)
            proj(20)
            level_t1(6)
            proj(21)
            level_pq(6)
            pe.wait_ge(sem("om_ready"), 1)
            pe.wait_ge(sem("inv_ready"), 5)
            transposes([om[:, t, h * P:(h + 1) * P] for h in range(H) for t in range(T)], (2, 3), "om_turned")
            proj(22)
            pe.wait_ge(sem("inv_ready"), 6)
            chunk_products(0, "u0_done", lambda h: (invT[:, h, 0, :], vb[:, h, 0, :]))
            proj(23)
            pe.wait_ge(sem("u0_ready"), 1)
            chunk_products(1, "state_done", lambda h: (kd0[:, h, :], ua[:, h, :]))
            chunk_products(4, "o0_done", lambda h: (attn[:, h, 0, :], ua[:, h, :]))

            def lift(i):
                j = UP_FIRST + i
                landed(pe, j)
                if i == 0:
                    pe.wait_ge(sem("proj_taken"), N_IN - CONV_PIECES)
                if i >= 1:
                    pe.wait_ge(sem("lift_taken"), i)
                src = cvm[:, 0:HC, :]
                w = slot3(j % RING, HC)
                for c in range(4):
                    for k in range(HC):
                        mm = pe.matmul(B[6 + c // 2][:, (c % 2) * S:(c % 2 + 1) * S], w[:, k, c * P:(c + 1) * P],
                                       src[:, k, :], start=(k == 0), stop=(k == HC - 1))
                mm.then_inc(sem("piece_done"), 1)

            def lift_chunk(i, t, banks):
                landed(pe, UP_FIRST + 2 + i)
                w = slot3((UP_FIRST + 2 + i) % RING, HC)
                for c in range(4):
                    for k in range(HC):
                        at = (c % 2) * S + t * P
                        mm = pe.matmul(B[banks[c // 2]][:, at:at + P], w[:, k, c * P:(c + 1) * P],
                                       cvg[:, 2 * HC + k, t * P:(t + 1) * P], start=(k == 0), stop=(k == HC - 1))
                if t == T - 1:
                    mm.then_inc(sem("piece_done"), 1)

            pe.wait_ge(sem("omT_ready"), 1)
            lift(0)
            pe.wait_ge(sem("state_ready"), 1)
            chunk_products(0, "ks_done", lambda h: (kT(h, 1), st[:, h, :]))
            chunk_products(1, "qs_done", lambda h: (qT(h, 1), st[:, h, :]))
            pe.wait_ge(sem("og_ready"), 1)
            transposes([og[:, 0, h * P:(h + 1) * P] for h in range(H)], (3,), "og_turned")
            lift(1)
            pe.wait_ge(sem("rhs1_ready"), 1)
            chunk_products(0, "u1_done", lambda h: (invT[:, h, 1, :], ub[:, h, :]))
            pe.wait_ge(sem("u1_ready"), 1)
            chunk_products(2, "au_done", lambda h: (attn[:, h, 1, :], ua[:, h, :]))
            pe.wait_ge(sem("ogT_ready"), 1)
            lift_chunk(1, 0, (4, 5))
            pe.wait_ge(sem("lift_taken"), 2)
            lift_chunk(0, 0, (6, 7))
            pe.wait_ge(sem("og_ready"), T)
            transposes([og[:, 1, h * P:(h + 1) * P] for h in range(H)], (2,), "og_turned")
            pe.wait_ge(sem("ogT_ready"), T)
            lift_chunk(0, 1, (6, 7))
            lift_chunk(1, 1, (4, 5))
            def out_product(i, k, t, n):
                kk = 2 * i + k
                return pe.matmul(B[2 * t + n], gate_g[:, kk, t * P:(t + 1) * P],
                                 slot3((OUT_FIRST + i) % RING, 2)[:, k, n * HALF:(n + 1) * HALF],
                                 start=(kk == 0), stop=(kk == KC - 1))

            for i in range(3):
                pe.wait_ge(sem("lift_taken"), 3 + i // 2)
                landed(pe, OUT_FIRST + i)
                for k in range(2):
                    for t in range(T):
                        for n in range(2):
                            mm = out_product(i, k, t, n)
                mm.then_inc(sem("piece_done"), 1)
            landed(pe, OUT_FIRST + 3)
            for t in range(T):
                for n in range(2):
                    for k in range(2):
                        mm = out_product(3, k, t, n)
                    mm.then_inc(sem("piece_done" if (t, n) == (T - 1, 1) else "out_bank_done"), 1)
            for t in range(T):
                pe.wait_ge(sem("x2_ready"), t + 1)
                transposes([xs[:, t, k * P:(k + 1) * P] for k in range(KC)], [4 + 2 * t, 5 + 2 * t], "x2_turned")
            pe.wait_ge(sem("tail_params"), 16 * 5)
            for t in range(T):
                pe.wait_ge(sem("x2T_ready"), 2 * (t + 1))
                for k in range(KC):
                    mm = pe.matmul(B[0][0:E, t * P:(t + 1) * P], wr[:, k, :], hT[:, k, t * P:(t + 1) * P],
                                   start=(k == 0), stop=(k == KC - 1))
            mm.then_inc(sem("logitsT_done"), 1)
            pe.wait_ge(sem("logitsT_ready"), 1)
            for t in range(T):
                mm = pe.transpose(B[1][:, t * E:(t + 1) * E], logitsT[:, t * P:(t + 1) * P], ident[0:E, 0:E])
            mm.then_inc(sem("logits_done"), 1)
            def gather(n, b):
                for k in range(KC // 2 * b, KC // 2 * (b + 1)):
                    for t in range(T):
                        mm = pe.matmul(B[6 + b][:, (k % 4) * P:(k % 4 + 1) * P], hn[:, t, k * P:(k + 1) * P],
                                       onehot[:, t, :], start=(t == 0), stop=(t == T - 1))
                mm.then_inc(sem("gathered"), 1)

            def open_gate_up(n, e):
                pe.wait_ge(sem("picked_ready"), n * 2 + 2)
                for half in range(2):
                    for side in range(2):
                        at = side * FE + half * HALF
                        pe.matmul(B[4 + half][side * SLOTS:(side + 1) * SLOTS, :], picked[:, e, :], bgu[:, at:at + HALF],
                                  start=True, stop=False, skip_group_check=True)

            def gate_up(n, e, local):
                first = isinstance(n, int) and e == 0
                if not first:
                    pe.wait_ge(sem("xT_ready"), n * 2 + 2)
                    pe.wait_ge(sem("gu_taken"), n * 2 + e)
                    open_gate_up(n, e)
                for k in range(KC):
                    if first and k % 4 == 0:
                        pe.wait_ge(sem("xT_ready"), k // 4 + 1)
                    landed_in_pair(pe, n, local + k)
                    for half in range(2):
                        for side in range(2):
                            at = side * FE + half * HALF
                            mm = pe.matmul(B[4 + half][side * SLOTS:(side + 1) * SLOTS, :], xT[:, k, e * SLOTS:(e + 1) * SLOTS],
                                           slot(n, local + k)[:, at:at + HALF], start=False, stop=(k == KC - 1),
                                           skip_group_check=True)
                    mm.then_inc(sem("piece_done"), 1)

            def down(n, local, first=0, end=8):
                if first == 0:
                    pe.wait_ge(sem("turned_copied"), n * 2)
                    pe.wait_ge(sem("xT_ready"), n * 2)
                for i in range(first, end, 2):
                    landed_in_pair(pe, n, local + i)
                    landed_in_pair(pe, n, local + i + 1)
                    for k in range(2):
                        block_ = i + k
                        col = (block_ % 4) * P + (block_ // 4) * SLOTS
                        for half in range(2):
                            for e in range(2):
                                mm = pe.matmul(B[6 + half][e * SLOTS:(e + 1) * SLOTS, :], actT[:, e, col:col + SLOTS],
                                               by_block(slot(n, local + i + e), 2)[:, k, half * HALF:(half + 1) * HALF],
                                               start=(i == 0 and k == 0), stop=(i == 6 and k == 1),
                                               skip_group_check=True)
                                if k == 1 and half == 1:
                                    mm.then_inc(sem("piece_done"), 1)

            def turn_act(n, e):
                pe.wait_ge(sem("act_ready"), n * 2 + (e + 1))
                for c in range(4):
                    mm = pe.transpose(B[6 + e][:, c * P:(c + 1) * P], act[:, e, c * P:(c + 1) * P], ident[:, :])
                mm.then_inc(sem("act_turned"), 1)

            def turn_weighted(n):
                pe.wait_ge(sem("weighted_ready"), n * (2 * T) + 2 * T)
                for t in range(T):
                    mm = pe.transpose(B[6][:, t * P:(t + 1) * P], weighted[:, t, :], ident[:, :])
                mm.then_inc(sem("weighted_turned"), 1)

            def scatter(n):
                pe.wait_ge(sem("y_copied"), n * 2)
                pe.wait_ge(sem("scat_ready"), n)
                for t in range(T):
                    for half in range(2):
                        mm = pe.matmul(B[2 * t + half], scat[:, t, :], ysb[:, half * HALF:(half + 1) * HALF],
                                       start=False, stop=False, skip_group_check=True)
                mm.then_inc(sem("scattered"), 1)

            pe.wait_ge(sem("expert_bias"), 16)
            open_gate_up(0, 0)
            pe.wait_ge(sem("chosen_ready"), 1)
            at = T * E
            pe.matmul(B[1][:, at:at + E], striu[:, :], chosen[:, 0, :], start=True, stop=True)
            pe.matmul(B[1][:, at + E:at + 2 * E], striu[:, :], chosen[:, 1, :], start=True, stop=False)
            pe.matmul(B[1][:, at + E:at + 2 * E], ones[:, :], chosen[:, 0, :], start=False,
                      stop=True).then_inc(sem("ranks_done"), 1)

            keep_busy(6)
            pe.wait_ge(sem("onehot_ready"), 2 * T)
            pe.wait_ge(sem("h2_ready"), T)
            gather(0, 0)
            gather(0, 1)
            pe.wait_ge(sem("gates_ready"), 1)
            for t in range(T):
                pe.transpose(B[0][0:E, t * P:(t + 1) * P], gates[:, t, :], ident[:, :])
            for t in range(T):
                pe.transpose(B[1][0:E, t * P:(t + 1) * P], lg[:, t, :], ident[:, :])
            for t in range(T):
                mm = pe.matmul(B[0][0:E, S:S + 1], chosen[:, t, :], ones[:, 0:1], start=(t == 0), stop=(t == T - 1))
            mm.then_inc(sem("counts_done"), 1)
            gate_up(0, 0, 0)
            pe.wait_ge(sem("again_ready"), 1)
            pe.matmul(B[0][0:E, S + 8:S + 8 + MORE], striu[0:E, 0:E], again[:, :], start=True, stop=True)
            pe.matmul(B[0][:, S + 16:S + 16 + MORE], ones[0:E, :], again[:, :], start=True, stop=True).then_inc(sem("order_done"), 1)
            gate_up(0, 1, 8)
            pe.wait_ge(sem("placed_ready"), 1)
            for t in range(T):
                pe.matmul(B[0][:, 32 + t * EXTRA:32 + (t + 1) * EXTRA], gatesT[:, t * P:(t + 1) * P], placed[:, :],
                          start=True, stop=True)
            for t in range(T):
                pe.matmul(B[0][:, 64 + t * EXTRA:64 + (t + 1) * EXTRA], rankT[:, t * P:(t + 1) * P], placed[:, :],
                          start=True, stop=False)
                pe.matmul(B[0][:, 64 + t * EXTRA:64 + (t + 1) * EXTRA], ones[0:E, :], shift[:, :], start=False, stop=True)
            pe.matmul(B[0][:, 96:96 + EXTRA], ecol[0:E, :].to_broadcast([E, P]), placed[:, :], start=True,
                      stop=True).then_inc(sem("extra_done"), 1)
            turn_act(0, 0)
            pe.wait_ge(sem("turned_copied"), 1)

            def next_pair(n):
                pe.wait_ge(sem("onehot_ready"), n * (2 * T) + 4 * T)
                gather(n + 1, 1)
                pe.wait_ge(sem("turned_copied"), n * 2 + 1)
                gather(n + 1, 0)
                pe.wait_ge(sem("xT_ready"), n * 2 + 3)
                turn_act(n, 1)
                pe.wait_ge(sem("xT_ready"), n * 2 + 4)
                turn_weighted(n)

            next_pair(0)
            pe.wait_ge(sem("items_ready"), 1)
            pairs, odd = pair_counts(pe)
            with pe.Fori(1, pairs) as n:
                gate_up(n, 0, 0)
                pe.wait_ge(sem("scat_ready"), n)
                down(n, 8)
                gate_up(n, 1, 16)
                pe.wait_ge(sem("y_copied"), n * 2)
                turn_act(n, 0)
                with pe.If(n < 2):
                    pe.wait_ge(sem("bdn_loaded"), 16)
                    for t in range(T):
                        for half in range(2):
                            pe.matmul(B[2 * t + half], gatesT[:, t * P:(t + 1) * P], bdn[:, half * HALF:(half + 1) * HALF],
                                      start=True, stop=False, skip_group_check=True)
                scatter(n)
                next_pair(n)

            with pe.If(odd < 1):
                pe.wait_ge(sem("scat_ready"), pairs)
                down(pairs, 0)
                pe.wait_ge(sem("y_copied"), pairs * 2)
                for t in range(T):
                    for half in range(2):
                        mm = pe.matmul(B[2 * t + half], scat[:, t, :], ysb[:, half * HALF:(half + 1) * HALF],
                                       start=False, stop=True, skip_group_check=True)
                    mm.then_inc(sem("sums_done"), 1)
            with pe.If(odd > 0):
                gate_up(pairs, 0, 0)
                pe.wait_ge(sem("scat_ready"), pairs)
                down(pairs, 8, 0, 2)
                pe.wait_ge(sem("act_ready"), pairs * 2 + 1)
                for c in range(4):
                    mm = pe.transpose(B[4][:, c * P:(c + 1) * P], act[:, 0, c * P:(c + 1) * P], ident[:, :])
                mm.then_inc(sem("act_turned"), 1)
                pe.wait_ge(sem("weighted_ready"), pairs * (2 * T) + 2 * T)
                for t in range(T):
                    mm = pe.transpose(B[5][:, t * P:(t + 1) * P], weighted[:, t, :], ident[:, :])
                mm.then_inc(sem("weighted_turned"), 1)
                down(pairs, 8, 2, 8)
                pe.wait_ge(sem("turned_copied"), pairs * 2 + 1)
                pe.wait_ge(sem("scat_ready"), pairs + 1)
                for i in range(4):
                    landed_in_pair(pe, pairs, 16 + i)
                    for k in range(2):
                        block_ = 2 * i + k
                        col = (block_ % 4) * P + (block_ // 4) * SLOTS
                        for half in range(2):
                            mm = pe.matmul(B[4 + half][half * SLOTS:(half + 1) * SLOTS, :], actT_left[:, col:col + SLOTS],
                                           by_block(slot(pairs, 16 + i), 2)[:, k, half * HALF:(half + 1) * HALF],
                                           start=(i == 0 and k == 0), stop=(i == 3 and k == 1),
                                           skip_group_check=True)
                    mm.then_inc(sem("piece_done"), 1)
                    if i == 1:
                        scatter(pairs)
                pe.wait_ge(sem("y_copied"), pairs * 2 + 2)
                for t in range(T):
                    for half in range(2):
                        rows_ = slice(half * SLOTS, (half + 1) * SLOTS)
                        mm = pe.matmul(B[2 * t + half], scat_left[rows_, t, :], ysb[rows_, half * HALF:(half + 1) * HALF],
                                       start=False, stop=True, skip_group_check=True)
                    mm.then_inc(sem("sums_done"), 1)

        @block.vector
        def _(dve):
            steps = [0]

            def link(ins):
                steps[0] += 1
                ins.then_inc(sem("dve_step"), 1)
                dve.wait_ge(sem("dve_step"), steps[0])

            def signal(ins, name):
                ins.then_inc(sem(name), 1)

            def bc(ap, shape):
                return ap.to_broadcast(shape)

            dve.memset(rstd[:, :], 1.0).then_inc(sem("root_warm"), 1)
            link(dve.memset(sbias[:, H:2 * H], 0.0))

            def mean_square(norm, t):
                dve.wait_ge(sem("x_squared"), norm * T + t + 1)
                dve.tensor_scalar(ss[:, t:t + 1], ss[:, t:t + 1], 1.0 / D, NORM_EPS, ALU.mult,
                                  ALU.add).then_inc(sem("mean_square_ready"), 1)

            def normalised(norm, t, done):
                dve.wait_ge(sem("root_ready"), norm * T + t + 1)
                link(dve.reciprocal(rstd[:, t:t + 1], rstd[:, t:t + 1]))
                dve.tensor_scalar(hn[:, t, :], xs[:, t, :], rstd[:, t:t + 1], None, ALU.mult).then_inc(sem(done), 1)

            dve.wait_ge(sem("prm_turned"), 1)
            link(dve.tensor_copy(prmT[:, :], B[4][:, 0:96]))
            for t in range(T):
                mean_square(0, t)
            for t in range(T):
                normalised(0, t, "hn_ready")
            for b in range(2 * T):
                dve.wait_ge(sem("h_turned"), b + 1)
                t, k = b // 2, 4 * (b % 2)
                signal(dve.tensor_tensor(hT[:, k:k + 4, t * P:(t + 1) * P], B[b].rearrange("p (k i) -> p k i", k=4),
                                         bc(prmT[:, 80 + k:84 + k].unsqueeze(2), [P, 4, P]), ALU.mult), "hT_ready")
            dve.wait_ge(sem("scal_rows_done"), 1)
            dve.tensor_copy(scal_rows, B[5][0:4 * H, 128:128 + S]).then_inc(sem("scal_rows_ready"), 1)
            dve.wait_ge(sem("scal_done"), 1)
            dve.wait_ge(sem("sbias_loaded"), 64)
            signal(dve.tensor_tensor(pre[:, :, :], B[5][:, 0:T * 4 * H].rearrange("p (t c) -> p t c", t=T),
                                     bc(sbias[:, :].unsqueeze(1), [P, T, 4 * H]), ALU.add), "pre_ready")
            dve.wait_ge(sem("pre_ready"), 1)
            signal(dve.tensor_copy(q8[:, :, 0:H], pre[:, :, 0:H]), "q8_ready")
            dve.wait_ge(sem("th_ready"), 1)
            signal(dve.tensor_scalar(q8[:, :, H:2 * H], th[:, :, H:2 * H], -GATE_SOFTCAP, None, ALU.mult), "q8_ready")
            dve.wait_ge(sem("q8_ready"), 2)
            dve.scalar_tensor_tensor(out=a8[:, :, :], in0=q8[:, :, :], scalar=-1.0, in1=q8[:, :, :],
                                     op0=ALU.mult, op1=ALU.max).then_inc(sem("a8_ready"), 1)

            conv_n = [0]

            def conv(j):
                for c in range(2):
                    i = 2 * j + c
                    if i < 2 * HC:
                        dst, col, stride = cvg[:, i, :], i, 3 * HC
                    elif i < 4 * HC:
                        dst, col, stride = cvm[:, i - 2 * HC, :], 3 * HC * TAPS + i - 2 * HC, 2 * HC
                    else:
                        dst, col, stride = cvg[:, i - 2 * HC, :], i - 2 * HC, 3 * HC
                    src = B[6 + j % 2][:, c * S:(c + 1) * S]
                    if c == 0:
                        dve.wait_ge(sem("conv_tap3"), 2 * j + 2)
                    for tap in (2, 1, 0):
                        d = TAPS - 1 - tap
                        w = prmT[:, col + tap * stride:col + tap * stride + 1]
                        ins = dve.scalar_tensor_tensor(out=dst[:, d:], in0=src[:, 0:S - d], scalar=w, in1=dst[:, d:],
                                                       op0=ALU.mult, op1=ALU.add)
                        if tap:
                            link(ins)
                        else:
                            ins.then_inc(sem("conv_done"), 1)

            dve.wait_ge(sem("softlog_ready"), 1)
            link(dve.scalar_tensor_tensor(out=g8[:, :, :], in0=q8[:, :, :], scalar=0.0, in1=e8[:, :, :],
                                          op0=ALU.max, op1=ALU.add))
            dve.scalar_tensor_tensor(out=g8[:, :, 0:H], in0=g8[:, :, 0:H], scalar=-1.0,
                                     in1=bc(alog[:, :].unsqueeze(1), [P, T, H]), op0=ALU.mult,
                                     op1=ALU.mult).then_inc(sem("log_decay_ready"), 1)
            dve.tensor_scalar(g8[:, :, H:2 * H], g8[:, :, H:2 * H], -1.0, None, ALU.mult).then_inc(sem("log_decay_ready"), 1)
            conv(0)
            conv(1)
            dve.wait_ge(sem("cum_done"), 1)
            cum = B[5][:, 64:64 + T * 2 * H].rearrange("p (t c) -> p t c", t=T)
            link(dve.tensor_copy(rowsrc[:, :, 0:H], cum[:, :, 0:H]))
            link(dve.tensor_copy(fcum[:, :, :], cum[:, :, H:2 * H]))
            link(dve.scalar_tensor_tensor(out=acol[:, :, :], in0=th[:, :, 0:H], scalar=GATE_SOFTCAP, in1=fcum[:, :, :],
                                          op0=ALU.mult, op1=ALU.subtract))
            link(dve.tensor_tensor(ex8[:, 0:H], B[5][:, 96:96 + H], rowsrc[:, 0, 0:H], ALU.subtract))
            dve.tensor_copy(ex8[:, H:2 * H], rowsrc[:, 1, 0:H]).then_inc(sem("row_source_ready"), 1)
            conv(2)
            dve.wait_ge(sem("rows_turned"), 1)
            link(dve.tensor_copy(rows[:, :], B[5][0:2 * H, 128:128 + S]))
            link(dve.tensor_copy(arow[:, :], B[4][0:H, 128:128 + S]))
            dve.tensor_tensor_scan(cmrow[:, :], arow[:, :], arow[:, :], 0.0, ALU.max, ALU.max).then_inc(sem("rows_ready"), 1)
            conv(3)

            def normed(first, root, const, done):
                dve.wait_ge(sem("roots_ready"), root)
                r = t1[:, :, :, :].rearrange("p h t i -> p h (t i)")
                link(dve.reciprocal(r, r))
                v = cvg[:, first:first + HC, :]
                dve.scalar_tensor_tensor(out=v, in0=v, scalar=const, in1=r, op0=ALU.mult,
                                         op1=ALU.mult).then_inc(sem(done), 1)

            normed(0, 1, QS, "q_normed")
            dve.wait_ge(sem("decay_spread"), 1)
            for h in range(H):
                for t in range(T):
                    ins = dve.tensor_scalar(decay[:, h, t, :], B[h // 2][:, (h % 2) * S + t * P:(h % 2) * S + (t + 1) * P],
                                            rowsrc[:, t, h:h + 1], 0.0, ALU.subtract, ALU.min)
            ins.then_inc(sem("decay_log"), 1)
            conv(4)
            dve.wait_ge(sem("decay_exp"), 1)
            dve.wait_ge(sem("masks_ready"), 2)
            d8 = decay[:, :, :, :].rearrange("p h t i -> p (h t) i")
            dve.tensor_tensor(d8, d8, bc(triu[:, :].unsqueeze(1), [P, H * T, P]), ALU.mult).then_inc(sem("decay_ready"), 1)
            dve.wait_ge(sem("runmax_turned"), 1)
            dve.scalar_tensor_tensor(out=dmin[:, :, :], in0=B[5][:, 480:480 + T * H].rearrange("p (t h) -> p t h", t=T),
                                     scalar=-1.0, in1=fcum[:, :, :], op0=ALU.mult, op1=ALU.subtract).then_inc(sem("dmin_ready"), 1)
            normed(HC, 2, 1.0, "k_normed")
            conv(5)
            dve.wait_ge(sem("runmax_spread"), 1)
            for h in range(H):
                src = B[4 + h // 2][:, (h % 2) * S:(h % 2 + 1) * S]
                link(dve.tensor_scalar(pt[:, h, 0:2, :].rearrange("p b i -> p (b i)"), src, acol[:, 0, h:h + 1], 0.0,
                                       ALU.subtract, ALU.max))
                ins = dve.tensor_scalar(pt[:, h, 2, :], src[:, P:S], acol[:, 1, h:h + 1], 0.0, ALU.subtract, ALU.max)
            ins.then_inc(sem("pt_log_ready"), 1)
            conv(6)
            dve.wait_ge(sem("k_normed"), 1)
            dve.wait_ge(sem("decay_ready"), 1)
            for b in range(2):
                dve.wait_ge(sem("kk_done"), b + 1)
                v = lt[:, 2 * b:2 * b + 2, :, :].rearrange("p h t i -> p (h t i)")
                link(dve.tensor_tensor(v, B[b], decay[:, 2 * b:2 * b + 2, :, :].rearrange("p h t i -> p (h t i)"), ALU.mult))
                dve.wait_ge(sem("beta_spread"), 1)
                link(dve.tensor_tensor(v, v, B[2 + b], ALU.mult))
            dve.wait_ge(sem("levels_ready"), len(LEVELS))
            l8 = lt[:, :, :, :].rearrange("p h t i -> p (h t) i")
            m8 = ltm[:, :, :, :].rearrange("p h t i -> p (h t) i")

            def mask_level(m):
                dve.tensor_tensor(m8, l8, bc(level[:, m, :].unsqueeze(1), [P, H * T, P]), ALU.mult).then_inc(sem("level_ready"), 1)

            mask_level(0)
            conv(7)
            for b in range(2):
                dve.wait_ge(sem("kq_done"), b + 1)
                ins = dve.tensor_tensor(attn[:, 2 * b:2 * b + 2, :, :].rearrange("p h t i -> p (h t i)"), B[4 + b],
                                        decay[:, 2 * b:2 * b + 2, :, :].rearrange("p h t i -> p (h t i)"), ALU.mult)
            ins.then_inc(sem("attn_ready"), 1)
            dve.wait_ge(sem("pt_exp"), 1)
            v = pt[:, :, 0:3:2, :]
            link(dve.tensor_tensor(v, v, bc(triu[:, :].unsqueeze(1).unsqueeze(1), [P, H, 2, P]), ALU.mult))
            conv(8)

            inv8 = inv[:, :, :, :].rearrange("p h t i -> p (h t) i")
            invT8 = invT[:, :, :, :].rearrange("p h t i -> p (h t) i")
            ib = bc(ident[:, :].unsqueeze(1), [P, H * T, P])
            link(dve.tensor_tensor(invT8, m8, ib, ALU.add))
            for b in range(2):
                dve.wait_ge(sem("t1_done"), b + 1)
                link(dve.tensor_tensor(inv8[:, 4 * b:4 * b + 4, :], B[b].rearrange("p (a i) -> p a i", a=4),
                                       ib[:, 0:4, :], ALU.add))
            mask_level(1)
            for h in range(H):
                dve.wait_ge(sem("ml_kq_done"), h + 1)
                w = pt[:, h, :, :].rearrange("p b i -> p (b i)")
                dve.scalar_tensor_tensor(out=w, in0=B[2 + h][:, 0:3 * P], scalar=QS, in1=w, op0=ALU.mult,
                                         op1=ALU.mult).then_inc(sem("pt_ready"), 1)
            conv(9)

            t18 = t1[:, :, :, :].rearrange("p h t i -> p (h t i)")
            invf = inv[:, :, :, :].rearrange("p h t i -> p (h t i)")
            invTf = invT[:, :, :, :].rearrange("p h t i -> p (h t i)")

            def level_dve(m, between=None):
                for b in range(2):
                    dve.wait_ge(sem("t1_done"), 2 * m + b + 1)
                    ins = dve.tensor_copy(t18[:, b * HALF:(b + 1) * HALF], B[b])
                    if b == 0:
                        link(ins)
                ins.then_inc(sem("t1_ready"), 1)
                if between:
                    between()
                if m < len(LEVELS) - 1:
                    for b in range(2):
                        dve.wait_ge(sem("p_done"), 2 * (m - 1) + b + 1)
                        v = invf[:, b * HALF:(b + 1) * HALF]
                        link(dve.tensor_tensor(v, v, B[2 + b], ALU.add))
                for b in range(2):
                    dve.wait_ge(sem("q_done"), 2 * (m - 1) + b + 1)
                    v = invTf[:, b * HALF:(b + 1) * HALF]
                    ins = dve.tensor_tensor(v, v, B[4 + b], ALU.add)
                    if b == 0:
                        link(ins)
                ins.then_inc(sem("inv_ready"), 1)
                if m < len(LEVELS) - 1:
                    dve.wait_ge(sem("inv_ready"), m)
                    mask_level(m + 1)

            level_dve(1)
            dve.wait_ge(sem("beta_ready"), 1)
            for b in range(2):
                dve.wait_ge(sem("v_turned"), b + 1)
                for hh in range(2):
                    h = 2 * b + hh
                    ins = dve.tensor_tensor(vb[:, h, :, :], B[b][:, hh * S:(hh + 1) * S].rearrange("p (t i) -> p t i", t=T),
                                            bc(rowsrc[:, :, H + h:H + h + 1], [P, T, P]), ALU.mult)
            ins.then_inc(sem("vb_ready"), 1)
            level_dve(2)
            dve.wait_ge(sem("k_turned"), 1)
            dve.wait_ge(sem("ex8_ready"), 1)
            dve.tensor_tensor(kd0[:, :, :], B[0].rearrange("p (h i) -> p h i", h=H),
                              bc(ex8[:, 0:H].unsqueeze(2), [P, H, P]), ALU.mult).then_inc(sem("kd_ready"), 1)
            level_dve(3)

            def mlstm_rows():
                dve.wait_ge(sem("ml_sums_done"), 1)
                dve.wait_ge(sem("dmin_exp"), 1)
                link(dve.tensor_copy(den[:, :, :], B[4][:, 0:T * H].rearrange("p (t h) -> p t h", t=T)))
                link(dve.scalar_tensor_tensor(out=den[:, :, :], in0=den[:, :, :], scalar=-1.0, in1=den[:, :, :],
                                              op0=ALU.mult, op1=ALU.max))
                link(dve.tensor_tensor(den[:, :, :], den[:, :, :], dmin[:, :, :], ALU.max))
                link(dve.reciprocal(den[:, :, :], den[:, :, :]))
                for t in range(T):
                    ins = dve.tensor_tensor(om[:, t, :].rearrange("p (h i) -> p h i", h=H),
                                            B[2 + t].rearrange("p (h i) -> p h i", h=H),
                                            bc(den[:, t, :].unsqueeze(2), [P, H, P]), ALU.mult)
                ins.then_inc(sem("ml_sums_taken"), 1)

            def head_norm(o, scratch, t, col):
                v = o[:, t, :]
                link(dve.tensor_tensor(scratch, v, v, ALU.mult))
                link(dve.tensor_reduce(ss[:, col:col + H], scratch.rearrange("p (h i) -> p h i", h=H), AX.X, ALU.add))

            level_dve(4, mlstm_rows)
            dve.wait_ge(sem("ml_sums_taken"), 1)
            for t in range(T):
                head_norm(om, scr, t, t * H)
            dve.tensor_scalar(ss[:, :], ss[:, :], 1.0 / DH, NORM_EPS, ALU.mult, ALU.add).then_inc(sem("ml_ms_ready"), 1)
            level_dve(5)
            dve.wait_ge(sem("ml_root"), 1)
            dve.wait_ge(sem("tail_params"), 16 * 5)

            def gated(o, t, norm, gate, done, signals):
                v = o[:, t, :]
                v3 = v.rearrange("p (h i) -> p h i", h=H)
                link(dve.tensor_tensor(v3, v3, bc(rstd[:, t * H:(t + 1) * H].unsqueeze(2), [P, H, P]), ALU.mult))
                link(dve.tensor_tensor(v3, v3, norm, ALU.mult))
                ins = dve.tensor_tensor(v, v, gate[:, t, :], ALU.mult)
                if signals:
                    ins.then_inc(sem(done), 1)
                else:
                    link(ins)

            link(dve.reciprocal(rstd[:, :], rstd[:, :]))
            dve.wait_ge(sem("proj_taken"), 6)
            for t in range(T):
                gated(om, t, mnorm[:, :].rearrange("p (h i) -> p h i", h=H), mo_s, "om_ready", t == T - 1)
            level_dve(6)
            for b in range(2):
                dve.wait_ge(sem("om_turned"), b + 1)
                ins = dve.tensor_copy(cvm[:, 2 * b:2 * b + 2, :].rearrange("p h i -> p (h i)"), B[2 + b])
                if b == 0:
                    link(ins)
            ins.then_inc(sem("omT_ready"), 1)
            dve.wait_ge(sem("u0_done"), 1)
            dve.tensor_copy(ua[:, :, :].rearrange("p h i -> p (h i)"), B[0]).then_inc(sem("u0_ready"), 1)
            dve.wait_ge(sem("state_done"), 1)
            dve.tensor_copy(st[:, :, :].rearrange("p h i -> p (h i)"), B[1]).then_inc(sem("state_ready"), 1)
            dve.wait_ge(sem("o0_done"), 1)
            link(dve.tensor_copy(og[:, 0, :], B[4]))

            def gdn_rows(t):
                head_norm(og, scr, t, t * H)
                v = ss[:, t * H:(t + 1) * H]
                dve.tensor_scalar(v, v, 1.0 / DH, NORM_EPS, ALU.mult, ALU.add).then_inc(sem("gdn_ms_ready"), 1)
                dve.wait_ge(sem("gdn_root"), t + 1)
                v = rstd[:, t * H:(t + 1) * H]
                link(dve.reciprocal(v, v))
                gated(og, t, bc(gnorm[:, :].unsqueeze(1), [P, H, DH]), z_s, "og_ready", True)

            def take_ogT(t):
                dve.wait_ge(sem("og_turned"), t + 1)
                dve.tensor_copy(cvg[:, 2 * HC:3 * HC, t * P:(t + 1) * P],
                                B[3 - t].rearrange("p (h i) -> p h i", h=H)).then_inc(sem("ogT_ready"), 1)

            gdn_rows(0)
            link(dve.tensor_tensor(acol[:, 0, :], ex8[:, H:2 * H], rowsrc[:, 1, H:2 * H], ALU.mult))

            def merge_m(i):
                dve.wait_ge(sem("piece_done"), UP_FIRST + i + 1)
                dve.wait_ge(sem("proj_taken"), N_IN - CONV_PIECES)
                for b in range(2):
                    v = gate_m[:, 4 * i + 2 * b:4 * i + 2 * b + 2, :].rearrange("p c s -> p (c s)")
                    ins = dve.tensor_tensor(v, v, B[6 + b], ALU.mult)
                    if b == 0:
                        link(ins)
                ins.then_inc(sem("lift_taken"), 1)

            merge_m(0)
            dve.wait_ge(sem("ks_done"), 1)
            k3 = B[0].rearrange("p (h i) -> p h i", h=H)
            link(dve.tensor_tensor(ub[:, :, :], k3, bc(acol[:, 0, :].unsqueeze(2), [P, H, P]), ALU.mult))
            dve.tensor_tensor(ub[:, :, :], vb[:, :, 1, :], ub[:, :, :], ALU.subtract).then_inc(sem("rhs1_ready"), 1)
            dve.wait_ge(sem("qs_done"), 1)
            og3 = og[:, 1, :].rearrange("p (h i) -> p h i", h=H)
            link(dve.tensor_tensor(og3, B[1].rearrange("p (h i) -> p h i", h=H),
                                   bc(ex8[:, H:2 * H].unsqueeze(2), [P, H, P]), ALU.mult))
            take_ogT(0)
            dve.wait_ge(sem("u1_done"), 1)
            dve.tensor_copy(ua[:, :, :].rearrange("p h i -> p (h i)"), B[0]).then_inc(sem("u1_ready"), 1)
            merge_m(1)
            dve.wait_ge(sem("au_done"), 1)
            link(dve.tensor_tensor(og[:, 1, :], og[:, 1, :], B[2], ALU.add))
            gdn_rows(1)
            take_ogT(1)
            dve.wait_ge(sem("lift_taken"), 2)
            for i in range(2):
                dve.wait_ge(sem("piece_done"), UP_FIRST + 2 + i + 1)
                for b in range(2):
                    at = slice(4 * i + 2 * b, 4 * i + 2 * b + 2)
                    v = gate_g[:, at, :].rearrange("p c s -> p (c s)")
                    link(dve.tensor_tensor(v, v, B[(6, 4)[i] + b], ALU.mult))
                    ins = dve.tensor_tensor(v, v, gate_m[:, at, :].rearrange("p c s -> p (c s)"), ALU.add)
                    if b == 0:
                        link(ins)
                ins.then_inc(sem("lift_taken"), 1)
            def residual(t, done, wait=None):
                for n in range(2):
                    if wait:
                        wait(2 * t + n)
                    v = xs[:, t, n * HALF:(n + 1) * HALF]
                    ins = dve.tensor_tensor(v, v, B[2 * t + n], ALU.add)
                    if n == 0:
                        link(ins)
                ins.then_inc(sem(done), 1)

            def out_bank(i):
                if i < 2 * T - 1:
                    dve.wait_ge(sem("out_bank_done"), i + 1)
                else:
                    dve.wait_ge(sem("piece_done"), MOE_FIRST)

            fw = lambda k, n, m: bc(prmT[:, 88 + k:88 + k + n].unsqueeze(2), [P, n, m])

            def take_x2T(t):
                for b in range(2 * t, 2 * t + 2):
                    dve.wait_ge(sem("x2_turned"), b + 1)
                    k = 4 * (b % 2)
                    dve.tensor_tensor(hT[:, k:k + 4, t * P:(t + 1) * P], B[4 + b].rearrange("p (k i) -> p k i", k=4),
                                      fw(k, 4, P), ALU.mult).then_inc(sem("x2T_ready"), 1)

            residual(0, "x2_ready", out_bank)
            mean_square(1, 0)
            residual(1, "x2_ready", out_bank)
            take_x2T(0)
            take_x2T(1)
            mean_square(1, 1)
            for t in range(T):
                normalised(1, t, "h2_ready")
            def make_onehot(n):
                for t in range(T):
                    for e in range(2):
                        dve.tensor_scalar(onehot[:, t, e * SLOTS:(e + 1) * SLOTS], siota[:, :],
                                          posx[:, t, bass.ds(n * 2 + e, 1)], None,
                                          ALU.is_equal).then_inc(sem("onehot_ready"), 1)

            def make_weighted(n, items=(0, 1)):
                for t in range(T):
                    for e in range(2):
                        dve.tensor_scalar(weighted[:, t, e * SLOTS:(e + 1) * SLOTS], siota[:, :],
                                          posx[:, t, bass.ds(n * 2 + items[e], 1)],
                                          gatex[:, t, bass.ds(n * 2 + items[e], 1)],
                                          ALU.is_equal, ALU.mult).then_inc(sem("weighted_ready"), 1)

            def make_picked(n):
                for e in range(2):
                    dve.tensor_copy(picked[:, e, :], bc(pick[:, bass.ds(n * 2 + e, 1)], [P, SLOTS])).then_inc(sem("picked_ready"), 1)

            def take_xT(n, b, count):
                dve.wait_ge(sem("gathered"), count)
                dve.tensor_tensor(xT[:, 4 * b:4 * b + 4, :], B[6 + b].rearrange("p (k s) -> p k s", k=4),
                                  fw(4 * b, 4, P), ALU.mult).then_inc(sem("xT_ready"), 1)

            def glu(n, e, wait):
                wait()
                if not isinstance(n, int) or e:
                    dve.wait_ge(sem("act_ready"), n * 2 + e)
                both = bank45[:, :, :].rearrange("p b (f two) -> p b f two", two=2)
                g2 = glu_g.rearrange("p (b f) -> p b f", b=2)
                u2 = glu_u.rearrange("p (b f) -> p b f", b=2)
                dve.tensor_scalar(g2, both[:, :, :, 0], SWIGLU_LIMIT, None, ALU.min).then_inc(sem("glu_g_ready"), 1)
                dve.tensor_scalar(u2, both[:, :, :, 1], SWIGLU_LIMIT, -SWIGLU_LIMIT, ALU.min,
                                  ALU.max).then_inc(sem("gu_taken"), 1)
                dve.wait_ge(sem("glu_g_ready"), n * 2 + (e + 1))
                dve.wait_ge(sem("gu_taken"), n * 2 + (e + 1))
                dve.scalar_tensor_tensor(out=glu_u, in0=glu_u, scalar=1.0, in1=glu_g, op0=ALU.add,
                                         op1=ALU.mult).then_inc(sem("glu_u_ready"), 1)
                dve.wait_ge(sem("glu_u_ready"), n * 2 + (e + 1))
                dve.wait_ge(sem("glu_s_ready"), n * 2 + (e + 1))
                dve.tensor_tensor(act[:, e, :], glu_u, glu_s, ALU.mult).then_inc(sem("act_ready"), 1)

            def take_scat(n):
                dve.wait_ge(sem("weighted_turned"), n + 1)
                dve.tensor_copy(scat.rearrange("p t i -> p (t i)"), B[6][:, 0:T * P]).then_inc(sem("scat_ready"), 1)

            def pieces(n, local):
                return lambda: dve.wait_ge(sem("piece_done"), pieces_before(n, local))

            dve.wait_ge(sem("tables_ready"), TABLES)
            make_picked(0)
            dve.wait_ge(sem("logitsT_done"), 1)
            dve.tensor_copy(logitsT, B[0][0:E, 0:S]).then_inc(sem("logitsT_ready"), 1)
            dve.wait_ge(sem("logits_done"), 1)
            for t in range(T):
                ins = dve.scalar_tensor_tensor(out=lg[:, t, :], in0=B[1][:, t * E:(t + 1) * E], scalar=rstd[:, t:t + 1],
                                               in1=brt[:, :], op0=ALU.mult, op1=ALU.add)
            link(ins)
            for t in range(T):
                ins = dve.max(mx8[:, t, :], lg[:, t, :])
            link(ins)
            for t in range(T):
                ins = dve.max_index(ix8[:, t, :], mx8[:, t, :], lg[:, t, :])
            link(ins)
            link(dve.tensor_copy(ixf[:, :, :], ix8[:, :, :]))
            link(dve.tensor_tensor(eq, bc(eiota[:, :].unsqueeze(1).unsqueeze(1), [P, T, TOP_K, E]),
                                   bc(ixf[:, :, 0:TOP_K].unsqueeze(3), [P, T, TOP_K, E]), ALU.is_equal))
            dve.tensor_reduce(chosen[:, :, :], eq.rearrange("p t j e -> p t e j"), AX.X, ALU.add).then_inc(sem("chosen_ready"), 1)
            dve.tensor_tensor(g4[:, :, :], mx8[:, :, 0:TOP_K], bc(mx8[:, :, 0:1], [P, T, TOP_K]),
                              ALU.subtract).then_inc(sem("top_ready"), 1)
            dve.memset(posx[:, :, E:], -1.0)
            link(dve.memset(gatex[:, :, E:], 0.0))
            dve.wait_ge(sem("chosen_ready"), 1)
            dve.wait_ge(sem("ranks_done"), 1)
            link(dve.scalar_tensor_tensor(out=lg[:, :, :], in0=B[1][:, T * E:2 * T * E].rearrange("p (t e) -> p t e", t=T),
                                          scalar=1.0, in1=chosen[:, :, :], op0=ALU.add, op1=ALU.mult))
            link(dve.tensor_scalar(posx[:, :, 0:E], lg[:, :, :], -1.0, None, ALU.add))
            make_onehot(0)
            dve.wait_ge(sem("top_exp"), 1)
            link(dve.tensor_reduce(gsum[:, :], g4[:, :, :], AX.X, ALU.add))
            link(dve.reciprocal(gsum[:, :], gsum[:, :]))
            link(dve.tensor_tensor(g4[:, :, :], g4[:, :, :], bc(gsum[:, :].unsqueeze(2), [P, T, TOP_K]), ALU.mult))
            link(dve.tensor_tensor(eq, eq, bc(g4[:, :, :].unsqueeze(3), [P, T, TOP_K, E]), ALU.mult))
            dve.tensor_reduce(gates[:, :, :], eq.rearrange("p t j e -> p t e j"), AX.X, ALU.add).then_inc(sem("gates_ready"), 1)
            take_xT(0, 0, 1)
            take_xT(0, 1, 2)
            dve.wait_ge(sem("gates_ready"), 1)
            link(dve.tensor_copy(gatex[:, :, 0:E], gates[:, :, :]))
            make_weighted(0)
            dve.wait_ge(sem("counts_done"), 1)
            link(dve.tensor_copy(gatesT, B[0][0:E, 0:S]))
            link(dve.tensor_copy(rankT, B[1][0:E, 0:S]))
            link(dve.tensor_copy(cntc[:, :], B[0][0:E, S:S + 1]))
            for r in range(MORE):
                ins = dve.tensor_scalar(again[:, r:r + 1], cntc[:, :], float((r + 1) * SLOTS), None, ALU.is_gt)
                if r < MORE - 1:
                    link(ins)
            ins.then_inc(sem("again_ready"), 1)
            make_onehot(1)
            glu(0, 0, lambda: dve.wait_ge(sem("piece_done"), MOE_FIRST + 8))
            dve.wait_ge(sem("order_done"), 1)
            link(dve.tensor_copy(order[:, :], B[0][0:E, S + 8:S + 8 + MORE]))
            link(dve.tensor_copy(totals[:, :], B[0][:, S + 16:S + 16 + MORE]))
            for r in range(MORE):
                for q in range(r):
                    link(dve.tensor_tensor(order[:, r:r + 1], order[:, r:r + 1], totals[0:E, q:q + 1], ALU.add))
            for r in range(MORE):
                link(dve.tensor_scalar(place[:, r, :], eiota[0:E, 0:EXTRA], order[:, r:r + 1], again[:, r:r + 1],
                                       ALU.is_equal, ALU.mult))
            link(dve.tensor_reduce(placed[:, :], place[:, :, :].rearrange("p r k -> p k r"), AX.X, ALU.add))
            link(dve.tensor_scalar(shift[:, :], place[:, 0, :], -float(SLOTS), None, ALU.mult))
            for r in range(1, MORE):
                ins = dve.scalar_tensor_tensor(out=shift[:, :], in0=place[:, r, :], scalar=-float((r + 1) * SLOTS),
                                               in1=shift[:, :], op0=ALU.mult, op1=ALU.add)
                if r < MORE - 1:
                    link(ins)
            ins.then_inc(sem("placed_ready"), 1)
            link(dve.tensor_reduce(cnt[:, 0:1], totals[:, :], AX.X, ALU.add))
            link(dve.tensor_scalar(cnt[:, 1:2], cnt[:, 0:1], -1.0, None, ALU.add))
            for c in range(2):
                link(dve.tensor_scalar(half_n[:, :], eiota[:, 0:EXTRA // 2], 2.0, cnt[:, c:c + 1], ALU.mult, ALU.is_lt))
                link(dve.tensor_reduce(cnt[:, 2 + c:3 + c], half_n[:, :], AX.X, ALU.add))
            link(dve.tensor_scalar(n_pairs[:, 0:1], cnt[:, 3:4], float(PAIRS), None, ALU.add))
            link(dve.tensor_tensor(n_pairs[:, 1:2], cnt[:, 2:3], cnt[:, 3:4], ALU.subtract))
            glu(0, 1, lambda: dve.wait_ge(sem("piece_done"), MOE_FIRST + 16))
            dve.wait_ge(sem("extra_done"), 1)
            x3 = lambda at: B[0][:, at:at + T * EXTRA].rearrange("p (t k) -> p t k", t=T)
            link(dve.tensor_copy(gatex[:, :, E:E + EXTRA], x3(32)))
            link(dve.tensor_scalar(posx[:, :, E:E + EXTRA], x3(64), -1.0, None, ALU.add))
            link(dve.tensor_copy(pick[0:E, E:E + EXTRA], placed[:, :]))
            link(dve.tensor_copy(ids[:, 0:E], eiota[0:1, :]))
            dve.tensor_copy(ids[:, E:E + EXTRA], B[0][0:1, 96:96 + EXTRA]).then_inc(sem("items_ready"), 1)
            dve.wait_ge(sem("items_ready"), 1)
            pairs, odd = pair_counts(dve)
            make_picked(1)
            take_xT(1, 1, 3)
            take_xT(1, 0, 4)
            take_scat(0)
            with dve.Fori(1, pairs) as n:
                dve.wait_ge(sem("gathered"), n * 2 + 2)
                make_onehot(n + 1)
                make_weighted(n)
                glu(n, 0, pieces(n, 8))
                glu(n, 1, pieces(n, 24))
                make_picked(n + 1)
                take_xT(n + 1, 1, n * 2 + 3)
                take_xT(n + 1, 0, n * 2 + 4)
                take_scat(n)
            with dve.If(odd > 0):
                make_weighted(pairs, (0, 0))
                glu(pairs, 0, pieces(pairs, 8))
                dve.wait_ge(sem("weighted_turned"), pairs + 1)
                dve.tensor_copy(scat_left.rearrange("p t i -> p (t i)"), B[5][:, 0:T * P]).then_inc(sem("scat_ready"), 1)
                dve.wait_ge(sem("piece_done"), pieces_before(pairs, 20))
                dve.wait_ge(sem("scattered"), pairs)
                dve.tensor_copy(ysb[SLOTS:P, HALF:D], B[5][SLOTS:P, :]).then_inc(sem("y_copied"), 1)
            for t in range(T):
                dve.wait_ge(sem("sums_done"), t + 1)
                residual(t, "x3_ready")
            for t in range(T):
                mean_square(2, t)
            for t in range(T):
                dve.wait_ge(sem("root_ready"), 2 * T + t + 1)
                link(dve.reciprocal(rstd[:, t:t + 1], rstd[:, t:t + 1]))
                dve.scalar_tensor_tensor(out=hn[:, t, :], in0=xs[:, t, :], scalar=rstd[:, t:t + 1], in1=fnorm[:, :],
                                         op0=ALU.mult, op1=ALU.mult).then_inc(sem("result_ready"), 1)

        @block.scalar
        def _(se):
            se.wait_ge(sem("root_warm"), 1)
            se.activation(rstd[:, :], rstd[:, :], ACT.Sqrt).then_inc(sem("root_warmed"), 1)
            se.dma_start(wsc[:, :, 0:2 * H], w_in_v[:, :, c_ga:c_ga + 2 * H]).then_inc(sem("scal_loaded"), 16)
            se.dma_start(wsc[:, :, 2 * H:4 * H], w_in_v[:, :, c_mi:c_mi + 2 * H]).then_inc(sem("scal_loaded"), 16)
            def squares(t):
                se.activation(hn[:, t, :], xs[:, t, :], ACT.Square, accum_out=ss[:, t:t + 1]).then_inc(sem("x_squared"), 1)

            def root(norm, t):
                se.wait_ge(sem("mean_square_ready"), norm * T + t + 1)
                se.activation(rstd[:, t:t + 1], ss[:, t:t + 1], ACT.Sqrt).then_inc(sem("root_ready"), 1)

            for t in range(T):
                se.wait_ge(sem(f"x{t}_loaded"), 16)
                squares(t)
            for t in range(T):
                root(0, t)
            se.dma_start(gnorm[:, :], gdn_norm.rearrange("l c -> (l c)").partition_broadcast(P)).then_inc(sem("tail_params"), 16)
            se.dma_start(mnorm[:, :], ml_norm.rearrange("l c -> (l c)").partition_broadcast(P)).then_inc(sem("tail_params"), 16)
            se.dma_start(brt[:, :], b_router.rearrange("l c -> (l c)").partition_broadcast(P)).then_inc(sem("tail_params"), 16)
            se.dma_start(fnorm[:, :], norm_final.partition_broadcast(P)).then_inc(sem("tail_params"), 16)
            se.dma_start(wr[:, :, :], w_router.rearrange("l (k p) e -> p (l k) e", p=P)).then_inc(sem("tail_params"), 16)
            se.wait_ge(sem("bgu_zeroed"), 1)
            se.dma_start(bgu[0:E, :], b_gate_up.rearrange("l e f -> (l e) f")).then_inc(sem("expert_bias"), 16)

            se.wait_ge(sem("pre_ready"), 1)
            se.activation(th[:, :, :], pre[:, :, 2 * H:4 * H], ACT.Tanh, scale=1.0 / GATE_SOFTCAP).then_inc(sem("th_ready"), 1)
            se.activation(rowsrc[:, :, H:2 * H], pre[:, :, H:2 * H], ACT.Sigmoid).then_inc(sem("beta_ready"), 1)
            se.wait_ge(sem("a8_ready"), 1)
            se.activation(e8[:, :, :], a8[:, :, :], ACT.Exp, scale=-1.0).then_inc(sem("e8_ready"), 1)
            se.activation(alog[:, :], alog[:, :], ACT.Exp).then_inc(sem("e8_ready"), 1)
            se.wait_ge(sem("e8_ready"), 2)
            se.activation(e8[:, :, :], e8[:, :, :], ACT.Ln, bias=1.0).then_inc(sem("softlog_ready"), 1)

            def tap3(j):
                se.wait_ge(sem("piece_done"), j + 1)
                for c in range(2):
                    i = 2 * j + c
                    if i < 2 * HC:
                        dst, col, stride = cvg[:, i, :], i, 3 * HC
                    elif i < 4 * HC:
                        dst, col, stride = cvm[:, i - 2 * HC, :], 3 * HC * TAPS + i - 2 * HC, 2 * HC
                    else:
                        dst, col, stride = cvg[:, i - 2 * HC, :], i - 2 * HC, 3 * HC
                    at = col + (TAPS - 1) * stride
                    se.activation(dst, B[6 + j % 2][:, c * S:(c + 1) * S], ACT.Identity,
                                  scale=prmT[:, at:at + 1]).then_inc(sem("conv_tap3"), 1)

            def conv_act(j):
                for c in range(2):
                    i = 2 * j + c
                    se.wait_ge(sem("conv_done"), i + 1)
                    dst = cvg[:, i, :] if i < 2 * HC else cvm[:, i - 2 * HC, :] if i < 4 * HC else cvg[:, i - 2 * HC, :]
                    ins = se.activation(dst, dst, ACT.Silu)
                    ins.then_inc(sem("conv_silu"), 1)

            def square(first, n):
                se.wait_ge(sem("conv_silu"), first + HC)
                se.activation(attn[:, :, :, :].rearrange("p h t i -> p h (t i)"), cvg[:, first:first + HC, :],
                              ACT.Square).then_inc(sem("squares_ready"), 1)

            def roots(n):
                se.wait_ge(sem("norm_sums"), n)
                if n == 2:
                    se.wait_ge(sem("q_normed"), 1)
                for b in range(2):
                    ins = se.activation(t1[:, 2 * b:2 * b + 2, :, :].rearrange("p h t i -> p (h t i)"), B[2 + b],
                                        ACT.Sqrt, bias=NORM_EPS)
                ins.then_inc(sem("roots_ready"), 1)

            tap3(0)
            tap3(1)
            conv_act(0)
            conv_act(1)
            square(0, 1)
            se.wait_ge(sem("row_source_ready"), 1)
            se.activation(ex8[:, :], ex8[:, :], ACT.Exp).then_inc(sem("ex8_ready"), 1)
            tap3(2)
            conv_act(2)
            tap3(3)
            roots(1)
            conv_act(3)
            square(HC, 2)
            se.wait_ge(sem("decay_log"), 1)
            se.activation(decay[:, :, :, :].rearrange("p h t i -> p (h t i)"),
                          decay[:, :, :, :].rearrange("p h t i -> p (h t i)"), ACT.Exp).then_inc(sem("decay_exp"), 1)
            tap3(4)
            roots(2)
            conv_act(4)
            tap3(5)
            se.wait_ge(sem("dmin_ready"), 1)
            se.activation(dmin[:, :, :], dmin[:, :, :], ACT.Exp).then_inc(sem("dmin_exp"), 1)
            conv_act(5)
            se.wait_ge(sem("pt_log_ready"), 1)
            se.activation(pt[:, :, :, :].rearrange("p h b i -> p (h b i)"), pt[:, :, :, :].rearrange("p h b i -> p (h b i)"),
                          ACT.Exp, scale=-1.0).then_inc(sem("pt_exp"), 1)
            tap3(6)
            conv_act(6)
            tap3(7)
            conv_act(7)
            se.wait_ge(sem("conv_silu"), 4 * HC)
            se.activation(gsum[:, 0:1], prmT[:, 0:1], ACT.Identity).then_inc(sem("mlstm_qk_ready"), 1)
            tap3(8)
            conv_act(8)
            tap3(9)
            conv_act(9)
            for j in range(CONV_PIECES, N_IN):
                se.wait_ge(sem("piece_done"), j + 1)
                if j < GATE_FIRST:
                    dst, func = ((mv_s, ACT.Identity), (z_s, ACT.Silu), (mo_s, ACT.Sigmoid))[(j - NAT_FIRST) // 2]
                    o = dst[:, :, (j % 2) * PW:(j % 2 + 1) * PW]
                    src = B[6 + j % 2].rearrange("p (t c) -> p t c", t=T)
                else:
                    i = j - GATE_FIRST
                    o = (gate_g if i < 4 else gate_m)[:, 2 * (i % 4):2 * (i % 4) + 2, :].rearrange("p c s -> p (c s)")
                    src, func = B[6 + j % 2], ACT.Sigmoid
                se.activation(o, src, func).then_inc(sem("proj_taken"), 1)
                if j == 18:
                    se.wait_ge(sem("ml_ms_ready"), 1)
                    se.activation(rstd[:, :], ss[:, :], ACT.Sqrt).then_inc(sem("ml_root"), 1)
            for t in range(T):
                se.wait_ge(sem("gdn_ms_ready"), t + 1)
                se.activation(rstd[:, t * H:(t + 1) * H], ss[:, t * H:(t + 1) * H], ACT.Sqrt).then_inc(sem("gdn_root"), 1)
            for t in range(T):
                se.wait_ge(sem("x2_ready"), t + 1)
                squares(t)
                root(1, t)
            se.wait_ge(sem("top_ready"), 1)
            se.activation(g4[:, :, :], g4[:, :, :], ACT.Exp).then_inc(sem("top_exp"), 1)

            def sigmoid(n, e):
                se.wait_ge(sem("glu_g_ready"), n * 2 + (e + 1))
                if isinstance(n, int):
                    if e:
                        se.wait_ge(sem("act_ready"), 1)
                else:
                    se.wait_ge(sem("act_ready"), n * 2 + e)
                se.activation(glu_s, glu_g, ACT.Sigmoid, scale=SWIGLU_ALPHA).then_inc(sem("glu_s_ready"), 1)

            def take_turned(n, e):
                se.wait_ge(sem("act_turned"), n * 2 + (e + 1))
                se.activation(actT[:, e, :], B[6 + e], ACT.Identity).then_inc(sem("turned_copied"), 1)

            def take_y(done):
                se.wait_ge(sem("piece_done"), done)
                for half in range(2):
                    se.activation(ysb[:, half * HALF:(half + 1) * HALF], B[6 + half], ACT.Identity).then_inc(sem("y_copied"), 1)

            se.wait_ge(sem("piece_done"), MOE_FIRST + 1)
            se.dma_start(bdn, b_down.rearrange("l e d -> (l e) d")).then_inc(sem("bdn_loaded"), 16)
            sigmoid(0, 0)
            sigmoid(0, 1)
            take_turned(0, 0)
            take_turned(0, 1)
            se.wait_ge(sem("items_ready"), 1)
            pairs, odd = pair_counts(se)
            with se.Fori(1, pairs) as n:
                sigmoid(n, 0)
                take_y(pieces_before(n, 16))
                sigmoid(n, 1)
                take_turned(n, 0)
                take_turned(n, 1)
            with se.If(odd < 1):
                take_y(pieces_before(pairs, 8))
            with se.If(odd > 0):
                sigmoid(pairs, 0)
                se.wait_ge(sem("act_turned"), pairs * 2 + 1)
                se.activation(actT_left, B[4], ACT.Identity).then_inc(sem("turned_copied"), 1)
                take_y(pieces_before(pairs, 16))
                se.wait_ge(sem("piece_done"), pieces_before(pairs, 20))
                se.wait_ge(sem("scattered"), pairs)
                se.activation(ysb[0:SLOTS, 0:HALF], B[4][0:SLOTS, :], ACT.Identity).then_inc(sem("y_copied"), 1)
            for t in range(T):
                se.wait_ge(sem("x3_ready"), t + 1)
                squares(t)
            for t in range(T):
                root(2, t)


_INS = ["x", "norm_mix", "w_in", "gdn_conv", "gdn_a_log", "gdn_dt_bias", "gdn_norm", "ml_conv", "ml_b_i", "ml_b_f",
        "ml_norm", "w_up_gdn", "w_up_ml", "w_out", "norm_ffn", "w_router", "b_router", "w_gate_up", "b_gate_up",
        "w_down", "b_down", "norm_final"]


def kernel(**inputs):
    import numpy as np
    import concourse.bacc as bacc
    from concourse.bass_utils import run_bass_kernel_spmd

    nc = bacc.Bacc("TRN2", target_bir_lowering=False, num_devices=1)
    arrays, args = {}, []
    for name in _INS:
        a = np.ascontiguousarray(inputs[name])
        arrays[f"in_{name}"] = a
        args.append(nc.dram_tensor(f"in_{name}", a.shape, mybir.dt.from_np(a.dtype), kind="ExternalInput").ap())
    out = nc.dram_tensor("out_0", inputs["x"].shape, F32, kind="ExternalOutput").ap()
    decoder_layer(nc, *args, out)
    r = run_bass_kernel_spmd(nc, [arrays], core_ids=[0])
    return r.results[0]["out_0"]
```
